# Optimizing a Trainium2 kernel written in Bass

```python
import math
import jax, jax.numpy as jnp
from jax import lax
import numpy as np

D_MODEL = 2048
BATCH = 1
SEQ = 256
DEPTH = 2

MEM_LEN = 256
ROPE_THETA = 500000.0
ROPE_FRAC = 4
NORM_EPS = 1e-6

GLA_HEADS = 4
GLA_DK = 64
GLA_DV = 128
GLA_GATE_RANK = 16
GLA_TAU = 16.0
GLA_CHUNK = 64

S5_GROUPS = 32
S5_CH = 16
S5_STATE = 64
S5_WIDTH = S5_GROUPS * S5_CH

DSA_HEADS = 4
DSA_HD = 128
DSA_IDX_HEADS = 16
DSA_IDX_DIM = 64
DSA_TOPK = 256
DSA_QBLOCK = 128

MEM_HEADS = 4
MEM_HD = 128

GLA_WIDTH = GLA_HEADS * GLA_DV
DSA_WIDTH = DSA_HEADS * DSA_HD
MEM_WIDTH = MEM_HEADS * MEM_HD
MIX_WIDTH = GLA_WIDTH + S5_WIDTH + DSA_WIDTH + MEM_WIDTH
OUT_HEAD_DIM = 128

IN_SPLITS = (GLA_HEADS * GLA_DK, GLA_HEADS * GLA_DK, GLA_WIDTH, GLA_GATE_RANK, GLA_WIDTH,
             S5_WIDTH, S5_WIDTH,
             DSA_WIDTH, DSA_HD, DSA_HD, DSA_IDX_HEADS * DSA_IDX_DIM, DSA_IDX_DIM, DSA_IDX_HEADS, DSA_WIDTH,
             MEM_WIDTH, MEM_WIDTH)
IN_WIDTH = sum(IN_SPLITS)

kernel_name = "hybrid_gla_s5_dsa_memxattn_trunk"

F32 = jnp.float32

def rms_norm(x, g):
    xf = x.astype(F32)
    y = xf * lax.rsqrt(jnp.mean(xf * xf, axis=-1, keepdims=True) + NORM_EPS)
    return y.astype(x.dtype) * g

def split_cols(p):
    idx, acc = [], 0
    for w in IN_SPLITS[:-1]:
        acc += w
        idx.append(acc)
    return jnp.split(p, idx, axis=-1)

def partial_rope(x, pos):
    d = x.shape[-1]
    rd = d // ROPE_FRAC
    half = rd // 2
    inv_freq = ROPE_THETA ** (-jnp.arange(half, dtype=F32) * 2.0 / rd)
    ang = pos.astype(F32)[:, :, None] * inv_freq
    cos = jnp.cos(ang)[:, :, None, :]
    sin = jnp.sin(ang)[:, :, None, :]
    xr = x[..., :rd].astype(F32)
    x1, x2 = xr[..., :half], xr[..., half:]
    rot = jnp.concatenate([x1 * cos - x2 * sin, x2 * cos + x1 * sin], axis=-1).astype(x.dtype)
    return jnp.concatenate([rot, x[..., rd:]], axis=-1)

def gla_chunked(q, k, v, log_a):
    B, S, H, dk = q.shape
    dv = v.shape[-1]
    C = GLA_CHUNK
    N = S // C
    q, k, v, log_a = (t.astype(F32).reshape(B, N, C, H, -1) for t in (q, k, v, log_a))
    b = jnp.cumsum(log_a, axis=2)
    b_last = b[:, :, -1]
    m = b[:, :, C // 2:C // 2 + 1]
    attn = jnp.einsum('bnthd,bnshd->bnhts', q * jnp.exp(b - m), k * jnp.exp(m - b))
    tril = jnp.tril(jnp.ones((C, C), dtype=bool))
    attn = jnp.where(tril, attn, 0.0)
    o_intra = jnp.einsum('bnhts,bnshe->bnthe', attn, v)
    d_state = jnp.einsum('bnshd,bnshe->bnhde', k * jnp.exp(b_last[:, :, None] - b), v)
    chunk_decay = jnp.exp(b_last)

    def step(state, inp):
        ds, dec = inp
        return dec[..., None] * state + ds, state

    _, s_prev = lax.scan(step, jnp.zeros((B, H, dk, dv), F32),
                         (jnp.moveaxis(d_state, 1, 0), jnp.moveaxis(chunk_decay, 1, 0)))
    s_prev = jnp.moveaxis(s_prev, 0, 1)
    o_inter = jnp.einsum('bnthd,bnhde->bnthe', q * jnp.exp(b), s_prev)
    return (o_intra + o_inter).reshape(B, S, H, dv)

def gla_branch(gq, gk, gv, glr, w_up, b_up):
    B, S, _ = gq.shape
    q = gq.reshape(B, S, GLA_HEADS, GLA_DK) * (GLA_DK ** -0.5)
    k = gk.reshape(B, S, GLA_HEADS, GLA_DK)
    v = gv.reshape(B, S, GLA_HEADS, GLA_DV)
    log_a = jax.nn.log_sigmoid((glr @ w_up + b_up).astype(F32)) / GLA_TAU
    log_a = log_a.reshape(B, S, GLA_HEADS, GLA_DK)
    o = gla_chunked(q, k, v, log_a)
    return o.reshape(B, S, GLA_WIDTH).astype(gq.dtype)

def s5_branch(u, a_re, a_im, log_step, b_re, b_im, c_re, c_im, d_skip, w_glu):
    B, S, _ = u.shape
    uf = u.astype(F32).reshape(B, S, S5_GROUPS, S5_CH)
    lam = lax.complex(a_re.astype(F32), a_im.astype(F32))
    step = jnp.exp(log_step.astype(F32))[:, None]
    lam_bar = jnp.exp(lam * step)
    b_bar = ((lam_bar - 1.0) / lam)[..., None] * lax.complex(b_re.astype(F32), b_im.astype(F32))
    bu = jnp.einsum('bsgc,gpc->bsgp', uf.astype(jnp.complex64), b_bar)
    a = jnp.broadcast_to(lam_bar, bu.shape)

    def combine(e1, e2):
        a1, b1 = e1
        a2, b2 = e2
        return a1 * a2, a2 * b1 + b2

    _, xs = lax.associative_scan(combine, (a, bu), axis=1)
    c = lax.complex(c_re.astype(F32), c_im.astype(F32))
    y = jnp.real(jnp.einsum('gcp,bsgp->bsgc', c, xs)) + d_skip.astype(F32).reshape(S5_GROUPS, S5_CH) * uf
    y = jax.nn.gelu(y.reshape(B, S, S5_WIDTH))
    y = y * jax.nn.sigmoid(y @ w_glu.astype(F32))
    return y.astype(u.dtype)

def dsa_branch(dq, dk, dv, diq, dik, diw, q_gain, k_gain, pos):
    B, S, _ = dq.shape
    k_sel = min(DSA_TOPK, S // 4)
    q = partial_rope(rms_norm(dq.reshape(B, S, DSA_HEADS, DSA_HD), q_gain), pos)
    k = partial_rope(rms_norm(dk.reshape(B, S, 1, DSA_HD), k_gain), pos)[:, :, 0]
    kv = jnp.concatenate([k, dv], axis=-1)
    iq = partial_rope(diq.reshape(B, S, DSA_IDX_HEADS, DSA_IDX_DIM), pos)
    ik = partial_rope(dik.reshape(B, S, 1, DSA_IDX_DIM), pos)[:, :, 0]
    iw = diw * (DSA_IDX_HEADS ** -0.5 * DSA_IDX_DIM ** -0.5)
    s_pos = jnp.arange(S)
    scale = DSA_HD ** -0.5

    def block(i):
        t0 = i * DSA_QBLOCK
        qb = lax.dynamic_slice_in_dim(q, t0, DSA_QBLOCK, axis=1)
        iqb = lax.dynamic_slice_in_dim(iq, t0, DSA_QBLOCK, axis=1)
        iwb = lax.dynamic_slice_in_dim(iw, t0, DSA_QBLOCK, axis=1)
        t_pos = t0 + jnp.arange(DSA_QBLOCK)
        rel = jax.nn.relu(jnp.einsum('bthd,bsd->bths', iqb, ik))
        score = jnp.einsum('bths,bth->bts', rel, iwb).astype(F32)
        causal = s_pos[None, :] <= t_pos[:, None]
        score = jnp.where(causal[None], score, -jnp.inf)
        _, idx = lax.top_k(score, k_sel)
        kv_sel = jax.vmap(lambda kk, ii: kk[ii])(kv, idx)
        ks, vs = kv_sel[..., :DSA_HD], kv_sel[..., DSA_HD:]
        valid = idx <= t_pos[None, :, None]
        logits = jnp.einsum('bthd,btkd->bhtk', qb, ks).astype(F32) * scale
        logits = jnp.where(valid[:, None], logits, -jnp.inf)
        p = jax.nn.softmax(logits, axis=-1).astype(vs.dtype)
        return jnp.einsum('bhtk,btkd->bthd', p, vs)

    out = lax.map(block, jnp.arange(S // DSA_QBLOCK))
    return jnp.moveaxis(out, 0, 1).reshape(B, S, DSA_WIDTH)

def mem_branch(mq, mem, mem_gain, w_kv, q_gain, k_gain):
    B, S, _ = mq.shape
    q = rms_norm(mq.reshape(B, S, MEM_HEADS, MEM_HD), q_gain)
    kv = rms_norm(mem, mem_gain) @ w_kv
    mk, mv = jnp.split(kv, 2, axis=-1)
    mk = rms_norm(mk.reshape(B, -1, MEM_HEADS, MEM_HD), k_gain)
    mv = mv.reshape(B, -1, MEM_HEADS, MEM_HD)
    logits = jnp.einsum('bthd,bmhd->bhtm', q, mk).astype(F32) * (MEM_HD ** -0.5)
    p = jax.nn.softmax(logits, axis=-1).astype(mv.dtype)
    return jnp.einsum('bhtm,bmhd->bthd', p, mv).reshape(B, S, MEM_WIDTH)

def setup_inputs(seed: int = 0) -> dict:
    key = jax.random.key(seed)
    ks = iter(jax.random.split(key, 40))
    L = DEPTH
    G, P, CH = S5_GROUPS, S5_STATE, S5_CH

    def nrm(shape, scale):
        return jax.random.normal(next(ks), shape, F32) * scale

    def gain(shape):
        return 1.0 + nrm(shape, 0.02)

    x = nrm((BATCH, SEQ, D_MODEL), 1.0)
    mem = nrm((BATCH, MEM_LEN, D_MODEL), 1.0)
    offset = jax.random.randint(next(ks), (BATCH, 1), 0, 4096, dtype=jnp.int32)
    positions = offset + jnp.arange(SEQ, dtype=jnp.int32)[None, :]
    ln_gain = gain((L, D_MODEL))
    w_in = nrm((L, D_MODEL, IN_WIDTH), D_MODEL ** -0.5)
    gla_w_up = nrm((L, GLA_GATE_RANK, GLA_HEADS * GLA_DK), GLA_GATE_RANK ** -0.5)
    gla_b_up = nrm((L, GLA_HEADS * GLA_DK), 0.1)
    s5_a_re = -0.5 + nrm((L, G, P), 0.01)
    s5_a_im = jnp.pi * jnp.arange(P, dtype=F32) + nrm((L, G, P), 0.01)
    s5_log_step = jax.random.uniform(next(ks), (L, G), F32, math.log(1e-3), math.log(1e-1))
    s5_b_re = nrm((L, G, P, CH), (2.0 * CH) ** -0.5)
    s5_b_im = nrm((L, G, P, CH), (2.0 * CH) ** -0.5)
    s5_c_re = nrm((L, G, CH, P), (2.0 * P) ** -0.5)
    s5_c_im = nrm((L, G, CH, P), (2.0 * P) ** -0.5)
    s5_d = nrm((L, S5_WIDTH), 1.0)
    s5_w_glu = nrm((L, S5_WIDTH, S5_WIDTH), S5_WIDTH ** -0.5)
    dsa_q_norm = gain((L, DSA_HD))
    dsa_k_norm = gain((L, DSA_HD))
    mem_norm = gain((L, D_MODEL))
    w_mem_kv = nrm((L, D_MODEL, 2 * MEM_WIDTH), D_MODEL ** -0.5)
    mem_q_norm = gain((L, MEM_HD))
    mem_k_norm = gain((L, MEM_HD))
    out_norm = gain((L, MIX_WIDTH))
    w_out = nrm((L, MIX_WIDTH, D_MODEL), (2.0 * DEPTH * MIX_WIDTH) ** -0.5)
    return {"x": x, "mem": mem, "positions": positions, "ln_gain": ln_gain, "w_in": w_in,
            "gla_w_up": gla_w_up, "gla_b_up": gla_b_up,
            "s5_a_re": s5_a_re, "s5_a_im": s5_a_im, "s5_log_step": s5_log_step,
            "s5_b_re": s5_b_re, "s5_b_im": s5_b_im, "s5_c_re": s5_c_re, "s5_c_im": s5_c_im,
            "s5_d": s5_d, "s5_w_glu": s5_w_glu,
            "dsa_q_norm": dsa_q_norm, "dsa_k_norm": dsa_k_norm,
            "mem_norm": mem_norm, "w_mem_kv": w_mem_kv, "mem_q_norm": mem_q_norm, "mem_k_norm": mem_k_norm,
            "out_norm": out_norm, "w_out": w_out}

def reference(x, mem, positions, ln_gain, w_in, gla_w_up, gla_b_up,
              s5_a_re, s5_a_im, s5_log_step, s5_b_re, s5_b_im, s5_c_re, s5_c_im, s5_d, s5_w_glu,
              dsa_q_norm, dsa_k_norm, mem_norm, w_mem_kv, mem_q_norm, mem_k_norm,
              out_norm, w_out):
    B, S, _ = x.shape
    n_out_heads = MIX_WIDTH // OUT_HEAD_DIM
    for l in range(DEPTH):
        h = rms_norm(x, ln_gain[l])
        p = h @ w_in[l]
        (gq, gk, gv, glr, gz, su, sz, dq, dk, dv, diq, dik, diw, dz, mq, mz) = split_cols(p)
        o_gla = gla_branch(gq, gk, gv, glr, gla_w_up[l], gla_b_up[l])
        o_s5 = s5_branch(su, s5_a_re[l], s5_a_im[l], s5_log_step[l], s5_b_re[l], s5_b_im[l],
                         s5_c_re[l], s5_c_im[l], s5_d[l], s5_w_glu[l])
        o_dsa = dsa_branch(dq, dk, dv, diq, dik, diw, dsa_q_norm[l], dsa_k_norm[l], positions)
        o_mem = mem_branch(mq, mem, mem_norm[l], w_mem_kv[l], mem_q_norm[l], mem_k_norm[l])
        o = jnp.concatenate([o_gla, o_s5, o_dsa, o_mem], axis=-1)
        o = rms_norm(o.reshape(B, S, n_out_heads, OUT_HEAD_DIM),
                     out_norm[l].reshape(n_out_heads, OUT_HEAD_DIM)).reshape(B, S, MIX_WIDTH)
        z = jnp.concatenate([gz, sz, dz, mz], axis=-1)
        x = x + (o * jax.nn.silu(z)) @ w_out[l]
    return x


_drawn_inputs = setup_inputs


def setup_inputs(seed=0):
    import zlib

    import numpy as np

    out = dict(_drawn_inputs(seed))
    spreads = {}
    factors = {'gla_b_up': 4.438,
     's5_a_re': 8.0,
     's5_a_im': 3.391,
     's5_log_step': 3.303,
     's5_b_re': 4.332,
     's5_b_im': 4.152,
     's5_c_re': 4.179,
     's5_c_im': 4.421,
     'dsa_q_norm': 8.0,
     'dsa_k_norm': 8.0,
     'mem_norm': 6.179,
     'mem_q_norm': 7.528,
     'mem_k_norm': 7.566,
     'out_norm': 4.972}
    for name, (base, spread) in spreads.items():
        noise = np.random.default_rng([zlib.crc32(name.encode()), seed]).standard_normal(out[name].shape)
        drawn = base * np.exp(spread * noise) if base else spread * noise
        out[name] = __import__('jax').numpy.asarray(drawn.astype(out[name].dtype))
    for name, factor in factors.items():
        out[name] = (out[name] * factor).astype(out[name].dtype)
    return out
```

```python
import math
from contextlib import ExitStack

import numpy as np
import concourse.bass as bass
from concourse import mybir

ALU = mybir.AluOpType
ACT = mybir.ActivationFunctionType
AX = mybir.AxisListType
F32 = mybir.dt.float32
F32R = mybir.dt.float32r
I32 = mybir.dt.int32

P = 128
L = 2
D = 2048
S = 256
NT = S // P
KT = D // P
W = 512
CK = 2
NC = KT // CK
GROUPS = 16
SLOTS = GROUPS * NC
PRO_GROUPS = 2 * L
PRO = PRO_GROUPS * NC
RING = 4
AHEAD = 3
EPS = 1e-6
H = 4
HD = 128
GD = 64
IH, ID = 16, 64
TOPK = 64
ST = 16
TB = 4
MAGIC = 1.5 * 2.0 ** 23
TWO_PI = 2 * math.pi
NEG = -3.0e38
TAKEN = -3.4e38
BIG = 1.0e30
IN = dict(gq=0, gk=256, gv=512, glr=1024, gz=1040, su=1552, sz=2064, dq=2576, dk=3088, dv=3216,
          iq=3344, ik=4368, iw=4432, dz=4448, mq=4960, mz=5472, end=5984)
MISC = dict(dk=0, dv=128, ik=256, iw=320, glr=336, end=352)
G_IQ0, G_IQ1, G_MISC, G_SU, G_DQ, G_GQK, G_GV, G_MQ, G_Z, G_OUT = 0, 1, 2, 3, 4, 5, 6, 7, 8, 12
B_DSA, B_GLA, B_S5, B_MEM = 0, 1, 2, 3
PC = dict(ln=0, on=16, are=32, aim=48, lst=64, d=80, mqg=84, qg=85, kg=213, bup=341, end=597)
MG = dict(mn=0, mk=16, end=17)

STEPS = [("iqT0", 12), ("iqT1", 13), ("iqT2", 20), ("iqT3", 21), ("ikT", 30), ("glrT", 31), ("gate", 32),
         ("uT0", 34), ("uT1", 35)]
STEPS += [(f"rel1_{i}", 36 + i) for i in range(8)] + [(f"rel0_{i}", 44 + i) for i in range(4)]
STEPS += [("qT0", 48), ("qT1", 49), ("lg1_0", 52), ("lg1_1", 53), ("cumD", 54), ("cumT", 55), ("lg0", 56),
          ("cumL", 57), ("dec", 58), ("pT1_0", 59), ("pT1_1", 60), ("pv1", 61), ("pT0", 62), ("pv0", 63),
          ("qeT", 64), ("keT", 65), ("qbT", 66), ("at0", 67), ("dS0", 68), ("dS1", 69), ("go0", 71),
          ("at1", 72), ("go1", 74), ("mqT0", 75), ("mqT1", 76), ("ml0_0", 77), ("ml0_1", 78), ("mp0_0", 80),
          ("mp0_1", 81), ("mv0", 82), ("ml1_0", 83), ("ml1_1", 84), ("yt0", 85), ("yt1", 86),
          ("mp1_0", 87), ("mp1_1", 88), ("mv1", 89), ("glu0", 90), ("glu1", 91)]
AT = {slot: name for name, slot in STEPS}
NUM = {name: n for n, (name, _) in enumerate(STEPS)}
NA = len(STEPS)
assert len(AT) == NA
PRO_A = 2 * L
S5_SLOT = [37 + (9 * j) // 4 for j in range(ST)]
S5_LAG = 4
BU = {s: j for j, s in enumerate(S5_SLOT)}
YS = {s + S5_LAG: j for j, s in enumerate(S5_SLOT)}
TURN_O = {89: 0, 90: 1, 91: 2, 92: 3, 97: 4, 98: 5, 100: 6, 101: 7}
TURN_N = {122 + c: c for c in range(6)}
TURN_X = {2: 6, 3: 7}
BX, BBU, BO, BN = 0, 2, 2 + ST, 2 + ST + 8
NB = BN + 6
SLOT = dict(STEPS)
XB = 3
TURN_P = {20: 0, 21: 1, 22: 2, 23: 3, 26: 4, 27: 5}
SQ_DQ, SQ_DSA, SQ_MQ, SQ_GLA, SQ_MEM, SQ_S5 = range(6)
SCALE = HD ** -0.5


def build(nc, stream, mem, x, pos, invf, mgain, par, bmat, cmat, wup, wglu, out):
    ctx = ExitStack()
    with ctx:
        top = [16640]
        placed = {}

        def at(name, shape, dt, offset=None):
            size = int(np.prod(shape[1:])) * 4
            if offset is None:
                offset = top[0]
                top[0] += (size + 31) // 32 * 32
            placed[name] = offset
            return nc.alloc_sbuf_tensor_at(name, shape, dt, offset=offset)

        raw = at("raw", [P, RING, CK * W], F32)
        whi = at("whi", [P, RING, CK * W], F32R)
        wlo = at("wlo", [P, RING, CK * W], F32R)
        hhi = at("hhi", [P, KT, S], F32R)
        hlo = at("hlo", [P, KT, S], F32R)
        tab = at("tab", [P, 2, 2, TB, S], F32)
        obuf = at("obuf", [P, 4, NT, W], F32)
        wg = at("wg", [P, 4, W], F32, placed["tab"])
        mhi = at("mhi", [P, KT, S], F32R, placed["tab"])
        mlo = at("mlo", [P, KT, S], F32R, placed["obuf"])
        iq = at("iq", [P, NT, IH * ID], F32, placed["obuf"])
        iqT = at("iqT", [P, IH // 2, S], F32, placed["obuf"] + 8192)
        P0 = at("P0", [P, H, P], F32, placed["obuf"] + 8192)
        P1 = at("P1", [P, H, S], F32, placed["obuf"] + 12288)
        xr = at("xr", [P, XB, NT, W], F32)
        uT = at("uT", [P, 4, S], F32)
        ych = at("ych", [P, 4, S], F32)
        kvT = at("kvT", [P, H, S], F32, placed["ych"])
        rot = at("rot", [P, 2, 2, S], F32)
        vz = at("vz", [P, 2, 2, S], F32)
        qq = at("qq", [P, 2, 2, S], F32)
        xs = at("xs", [P, 2, 2, S], F32)
        ytmp = at("ytmp", [P, S], F32)
        gt = at("gt", [P, NT, W], F32, placed["rot"])
        bm = at("bm", [P, 4, 2, P], F32)
        cp = at("cp", [P, ST, 2, 32], F32)
        pa = at("pa", [P, PC["end"]], F32)
        wu = at("wu", [16, S], F32)
        E1 = at("E1", [P, NT, W], F32)
        E2 = at("E2", [P, NT, W], F32)
        Pm = at("Pm", [P, H, S], F32, placed["E2"])
        E3 = at("E3", [P, NT, W], F32)
        la = at("la", [P, NT, S], F32)
        kkT = at("kkT", [P, 2, S], F32)
        Ez = at("Ez", [P, NT, W], F32, placed["la"])
        memr = at("memr", [P, NT, D], F32, placed["E1"])
        assert placed["la"] == placed["E1"] + 12288
        R1 = at("R1", [P, 2, W], F32)
        rel = R1
        pT = at("pT", [P, H, NT, P], F32, placed["R1"])
        R2 = at("R2", [P, H, S], F32)
        qT = R2
        qeT = at("qeT", [P, 2, S], F32, placed["R2"])
        keT = at("keT", [P, 2, S], F32, placed["R2"] + 2048)
        qbT = at("qbT", [P, 2, S], F32)
        t1 = at("t1", [P, NT, S], F32, placed["xr"])
        t2 = at("t2", [P, NT, S], F32, placed["xr"] + 2048)
        t3 = at("t3", [P, NT, S], F32, placed["xr"] + 4096)
        kd = at("kd", [P, NT, S], F32, placed["xr"] + 6144)
        mqT = at("mqT", [P, H, S], F32, placed["t1"])
        mkT = at("mkT", [P, H, S], F32, placed["t3"])
        mv = at("mv", [P, NT, W], F32, placed["E1"])
        sc = at("sc", [P, S], F32)
        sc0 = at("sc0", [P, P], F32)
        bias1 = at("bias1", [P, S], F32)
        bias0 = at("bias0", [P, P], F32)
        stt_ = at("Sst", [P, 3, 2, P], F32, placed["xr"] + 8192)
        attn = at("attn", [P, H, P], F32)
        misc = at("misc", [P, NT, MISC["end"]], F32)
        ikd = at("ikd", [P, NT, P], F32)
        rt = at("rt", [P, 4, NT * 8 * 8], F32)
        ident = at("ident", [P, P], F32)
        c01 = at("c01", [P, S], F32)
        negm = at("negm", [P, S], F32)
        tri = at("tri", [P, P], F32)
        triM = at("triM", [P, P], F32)
        triL = at("triL", [P, P], F32)
        cind = at("cind", [P, 2], F32)
        tvec = at("tvec", [P, S], F32)
        tint = at("tint", [P, S], I32, placed["vz"])
        mg = at("mg", [P, L, MG["end"]], F32)
        frq = at("frq", [P, 24], F32)
        posi = at("posi", [P, NT], I32)
        posf = at("posf", [P, NT], F32)
        ang = at("ang", [P, 4, NT, 24], F32, placed["qq"])
        snc = at("snc", [P, 2, NT, 24], F32)
        half = at("half", [P, 8], F32)
        ssx = at("ssx", [P, NT, 4], F32)
        rs = at("rs", [P, NT], F32)
        rsh = at("rsh", [P, NT], F32)
        ssm = at("ssm", [P, NT, 4], F32)
        rm = at("rm", [P, NT], F32)
        sq8 = at("sq8", [P, 8], F32)
        r8 = at("r8", [P, 8], F32)
        sqk = at("sqk", [P, NT], F32)
        rk = at("rk", [P, NT], F32)
        mx8 = at("mx8", [P, 8], F32)
        nm1 = at("nm1", [P, H], F32)
        nm0 = at("nm0", [P, H], F32)
        su1 = at("su1", [P, H], F32)
        su0 = at("su0", [P, H], F32)
        ri = at("ri", [P, H], F32)
        s5 = at("s5", [P, 16, ST], F32)
        dec = at("dec", [P, 2, 4], F32)
        assert top[0] <= 229368, top[0]

        acc = [[ctx.enter_context(nc.psum_tensor(f"acc{g}{t}", [P, W], F32)) for t in range(NT)] for g in range(2)]
        bankA = [ctx.enter_context(nc.psum_tensor(f"bankA{i}", [P, W], F32)) for i in range(2)]
        bankB = ctx.enter_context(nc.psum_tensor("bankB", [P, W], F32))
        bankY = ctx.enter_context(nc.psum_tensor("bankY", [P, 2, S], F32))

        kvs = nc.dram_tensor("kvs", [L, 2, P, 1024], F32, kind="Internal").ap()
        xsc = nc.dram_tensor("xsc", [P, NT, D], F32, kind="Internal").ap()

        counts = {}

        def sem(name, pro, per):
            s = ctx.enter_context(nc.semaphore(name))
            counts[s.name] = (pro, per)
            return s

        landed = [sem(f"landed{i}", 16 * PRO // RING, 16 * SLOTS // RING) for i in range(RING)]
        hi_done = sem("hi_done", PRO, SLOTS)
        lo_done = sem("lo_done", PRO, SLOTS)
        used = sem("used", PRO, SLOTS)
        taken = sem("taken", PRO_GROUPS, 8)
        gated = sem("gated", 0, 4)
        added = sem("added", 0, 4)
        stepped = sem("stepped", PRO_A, NA)
        freeA = [sem(f"freeA{i}", PRO_A // 2, NA // 2) for i in range(2)]
        wroteB = sem("wroteB", 22, NB)
        turned_hi = sem("turned_hi", 22, 16)
        freeB = sem("freeB", 22, NB)
        par_in = sem("par_in", 0, 64)
        glu_in = sem("glu_in", 0, 16)
        mk_in = sem("mk_in", 0, 16)
        mv_in = sem("mv_in", 0, 16)
        x_in = sem("x_in", 64, 64)
        x_out = sem("x_out", 0, 64)
        k_out = [sem(f"k_out{i}", 16, 0) for i in range(L)]
        v_out = [sem(f"v_out{i}", 16, 0) for i in range(L)]
        mem_in = sem("mem_in", 16, 0)
        const_in = sem("const_in", 48, 0)
        consts = sem("consts", 1, 0)
        ang_ready = sem("ang_ready", 1, 0)
        rope_ready = sem("rope_ready", 1, 0)
        sq_mem = sem("sq_mem", 1, 0)
        rm_sum = sem("rm_sum", 1, 0)
        rm_done = sem("rm_done", 1, 0)
        sq_kv = sem("sq_kv", L, 0)
        kv_sum = sem("kv_sum", L, 0)
        kv_norm = sem("kv_norm", L, 0)
        sq_x = sem("sq_x", 3, 4)
        rs_sum = sem("rs_sum", 0, 1)
        rs_done = sem("rs_done", 0, 1)
        roped_iq = sem("roped_iq", 0, 2)
        k_sum = sem("k_sum", 0, 1)
        roped_k = sem("roped_k", 0, 1)
        roped_q = sem("roped_q", 0, 1)
        weighed = sem("weighed", 0, 12)
        biased1 = sem("biased1", 0, 1)
        biased0 = sem("biased0", 0, 1)
        exp1 = sem("exp1", 0, 1)
        exp0 = sem("exp0", 0, 1)
        mmax = sem("mmax", 0, 4)
        lsoft = sem("lsoft", 0, 1)
        lsum = sem("lsum", 0, 1)
        gmul = sem("gmul", 0, 3)
        squared = sem("squared", 0, 6)
        sq_read = sem("sq_read", 0, 6)
        normr = sem("normr", 0, 6)
        obr = sem("obr", 0, 1)
        s5_exp = sem("s5_exp", 0, 1)
        s5_phase = sem("s5_phase", 0, 1)
        s5_sin = sem("s5_sin", 0, 1)
        s5_c = sem("s5_c", 0, 1)
        frac = sem("frac", 0, 4)
        phased = sem("phased", 0, 4)
        scanned = sem("scanned", 0, ST)
        unrot = sem("unrot", 0, ST)
        yprod = sem("yprod", 0, ST)
        ypoly = sem("ypoly", 0, 4)
        ytanh = sem("ytanh", 0, 4)
        gelud = sem("gelud", 0, 4)
        ztanh = sem("ztanh", 0, 4)
        zmul = sem("zmul", 0, 4)
        dve_own = sem("dve_own", 0, 0)
        act_own = sem("act_own", 0, 0)
        pe_own = sem("pe_own", 0, 0)
        pool_own = sem("pool_own", 0, 0)

        def counter(l):
            def upto(s, n):
                before, each = counts[s.name]
                return n if l is None else before + l * each + n
            return upto

        def linker(eng, s):
            count = [0]

            def link(ins):
                count[0] += 1
                ins.then_inc(s, 1)
                eng.wait_ge(s, count[0])
            return link

        def col(name, i=0):
            return pa[:, PC[name] + i:PC[name] + i + 1]

        def result(upto, name):
            s = freeA[NUM[name] % 2]
            return s, upto(s, NUM[name] // 2 + 1)

        assert NA % 2 == 0

        def bank_of(name):
            return bankA[NUM[name] % 2]

        block = ctx.enter_context(nc.Block())

        @block.sync
        def _(sp):
            xv = x.rearrange("(t p) d -> p t d", p=P)
            ov = out.rearrange("(t p) d -> p t d", p=P)

            def flat(t):
                return t[:].rearrange("p a b -> p (a b)")

            def chunk(n, l):
                upto = counter(l)
                if l is not None or n >= RING:
                    sp.wait_ge(hi_done, upto(hi_done, n - RING + 1))
                    sp.wait_ge(lo_done, upto(lo_done, n - RING + 1))
                total = n if l is None else PRO + SLOTS * l + n
                sp.dma_start(raw[:, n % RING, :], stream[total]).then_inc(landed[n % RING], 16)

            def params(l):
                if l >= 1:
                    sp.wait_ge(freeB, counter(l - 1)(freeB, BO + 8))
                sp.dma_start(pa[:], par[l]).then_inc(par_in, 16)
                sp.dma_start(bm[:], bmat[l]).then_inc(par_in, 16)
                sp.dma_start(cp[:], cmat[l]).then_inc(par_in, 16)
                sp.dma_start(wu[:], wup[l]).then_inc(par_in, 16)

            def x_load(l, g):
                src = xv if not l else xsc
                sp.dma_start(xr[:, g % XB], src[:, :, g * W:(g + 1) * W]).then_inc(x_in, 16)

            def x_store(l, g):
                sp.wait_ge(added, counter(l)(added, g + 1))
                dst = ov if l == L - 1 else xsc
                sp.dma_start(dst[:, :, g * W:(g + 1) * W], xr[:, g % XB]).then_inc(x_out, 16)

            def x_load3(l):
                upto = counter(l)
                sp.wait_ge(x_out, upto(x_out, 48))
                if l + 1 < L:
                    sp.wait_ge(wroteB, upto(wroteB, BN + 2))
                    sp.wait_ge(sq_x, upto(sq_x, 2))
                x_load(l, 3)

            upto = counter(None)
            sp.dma_start(memr[:], mem.rearrange("(t p) d -> p t d", p=P)).then_inc(mem_in, 16)
            sp.dma_start(mg[:], mgain).then_inc(const_in, 16)
            sp.dma_start(frq[:], invf.partition_broadcast(P)).then_inc(const_in, 16)
            sp.dma_start(posi[:], pos).then_inc(const_in, 16)
            for n in range(RING):
                chunk(n, None)
            params(0)
            for g in range(3):
                x_load(None, g)
            for n in range(RING, PRO):
                chunk(n, None)
                if n == 22:
                    sp.wait_ge(freeA[1], upto(freeA[1], 1))
                    sp.dma_start(kvs[0, 0], flat(kvT)).then_inc(k_out[0], 16)
                if n == 25:
                    sp.wait_ge(taken, upto(taken, 2))
                    sp.dma_start(kvs[0, 1], flat(R1)).then_inc(v_out[0], 16)
                if n == 30:
                    sp.wait_ge(wroteB, upto(wroteB, 18))
                    sp.wait_ge(sq_x, upto(sq_x, 1))
                    x_load(None, 3)
            for l in range(L):
                upto = counter(l)
                for n in range(SLOTS):
                    chunk(n, l)
                    if n == 3 and l > 0:
                        x_load3(l - 1)
                    if n == 6 and l == 0:
                        sp.wait_ge(freeA[1], counter(None)(freeA[1], 2))
                        sp.dma_start(kvs[1, 0], flat(kvT)).then_inc(k_out[1], 16)
                    if n == 10 and l == 0:
                        sp.wait_ge(taken, counter(None)(taken, 4))
                        sp.dma_start(kvs[1, 1], flat(R1)).then_inc(v_out[1], 16)
                    if n == 10 and l > 0:
                        x_store(l - 1, 3)
                    if n == 102:
                        sp.wait_ge(stepped, upto(stepped, NUM["ml1_1"] + 1))
                        if l > 0:
                            sp.wait_ge(x_out, upto(x_out, 0))
                        for g in range(3):
                            x_load(l, g)
                    if n == 82:
                        sp.wait_ge(k_out[l], 16)
                        sp.wait_ge(stepped, upto(stepped, NUM["dS1"] + 1))
                        sp.dma_start(flat(mkT), kvs[l, 0]).then_inc(mk_in, 16)
                    if n == 84:
                        sp.wait_ge(stepped, upto(stepped, NUM["go1"] + 1))
                        sp.wait_ge(v_out[l], 16)
                        sp.dma_start(flat(mv), kvs[l, 1]).then_inc(mv_in, 16)
                    if n == 88:
                        sp.wait_ge(unrot, upto(unrot, ST))
                        sp.dma_start(flat(wg), wglu[l]).then_inc(glu_in, 16)
                    if n == 113 and l + 1 < L:
                        params(l + 1)
                    if n in (112, 120):
                        x_store(l, (n - 112) // 8)
                    if n == 2 and l > 0:
                        x_store(l - 1, 2)
            x_store(L - 1, 2)
            x_load3(L - 1)
            x_store(L - 1, 3)
            sp.wait_ge(x_out, 64 * L)

        @block.gpsimd
        def _(pool):
            link = linker(pool, pool_own)
            upto = counter(None)
            g = nc.gpsimd
            for z in (ident, tri, triM, triL, cind, attn):
                g.memset(z[:], 0.0)
            g.memset(c01[:], 1.0)
            g.memset(half[:], -0.5)
            link(g.iota(tint[:], [[1, S]], base=0, channel_multiplier=0))
            link(g.tensor_copy(tvec[:], tint[:]))
            link(g.affine_select(out=ident[:], in_=ident[:], compare_op=ALU.not_equal, fill=1.0, base=0,
                                 pattern=[[-1, P]], channel_multiplier=1))
            link(g.affine_select(out=c01[:], in_=c01[:], compare_op=ALU.is_ge, fill=0.0, base=P,
                                 pattern=[[-1, S]], channel_multiplier=1))
            link(g.tensor_scalar(negm[:], c01[:], 1.0, -NEG, ALU.subtract, ALU.mult))
            link(g.affine_select(out=tri[:], in_=tri[:], compare_op=ALU.is_gt, fill=1.0, base=0,
                                 pattern=[[-1, P]], channel_multiplier=1))
            link(g.memset(tri[0:GD, GD:P], 0.0))
            for c in range(2):
                a = GD * c
                g.memset(triM[a:a + GD // 2 + 1, a:a + GD], 1.0)
                g.memset(triL[a:a + GD, a:a + GD], 1.0)
                link(g.memset(cind[a:a + GD, c:c + 1], 1.0))
            link(g.tensor_tensor(triM[:], tri[:], triM[:], ALU.subtract))
            g.tensor_tensor(triL[:], triL[:], tri[:], ALU.subtract).then_inc(consts, 1)

            def rstd(out_, in_, n, width):
                link(g.tensor_scalar(out_, in_, 1.0 / n, EPS, ALU.mult, ALU.add))
                return g.tensor_tensor(out_, out_, half[:, 0:width], ALU.pow)

            pool.wait_ge(const_in, upto(const_in, 48))
            link(g.tensor_copy(posf[:], posi[:]))
            for t in range(NT):
                link(g.tensor_scalar(ang[:, 3, t, :], frq[:], posf[:, t:t + 1], None, ALU.mult))
            c1 = 6.28125
            c2 = float(np.float32(np.round((TWO_PI - c1) * 2 ** 19) / 2 ** 19))
            c3 = TWO_PI - c1 - c2
            for i in range(2):
                link(g.tensor_scalar(ang[:, 2], ang[:, 3], 1.0 / TWO_PI, 0.25 * i, ALU.mult, ALU.add))
                link(g.tensor_scalar(ang[:, 2], ang[:, 2], MAGIC, None, ALU.add))
                link(g.tensor_scalar(ang[:, 2], ang[:, 2], MAGIC, None, ALU.subtract))
                first = True
                for c in (c1, c2, c3):
                    link(g.tensor_scalar(snc[:, 0], ang[:, 2], -c, None, ALU.mult))
                    link(g.tensor_tensor(ang[:, i], ang[:, 3] if first else ang[:, i], snc[:, 0], ALU.add))
                    first = False
                link(g.tensor_scalar(ang[:, i], ang[:, i], 0.5 * math.pi * i, 3.1415925, ALU.add, ALU.min))
                link(g.tensor_scalar(ang[:, i], ang[:, i], -3.1415925, None, ALU.max))
            g.tensor_copy(ang[:, 2], ang[:, 3]).then_inc(ang_ready, 1)

            pool.wait_ge(rm_sum, upto(rm_sum, 1))
            rstd(rm[:], rm[:], D, 2).then_inc(rm_done, 1)
            for l in range(L):
                pool.wait_ge(kv_sum, upto(kv_sum, l + 1))
                link(rstd(r8[:], sq8[:], HD, 8))
                kv = R2[:].rearrange("p a b -> p (a b)").rearrange("p (n d) -> p n d", d=HD)
                g.tensor_tensor(kv, kv, r8[:].unsqueeze(2).to_broadcast([P, 8, HD]), ALU.mult).then_inc(kv_norm, 1)

            def rope(v, tile0, heads, hf, f0, last):
                n = heads * hf

                def rv(i):
                    return rt[:, i, 0:NT * n].rearrange("p (t h f) -> p t h f", t=NT, h=heads)
                x1, x2 = v[:, :, :, 0:hf], v[:, :, :, hf:2 * hf]
                sn = snc[:, 0, :, f0:f0 + hf].unsqueeze(2).to_broadcast([P, NT, heads, hf])
                cs = snc[:, 1, :, f0:f0 + hf].unsqueeze(2).to_broadcast([P, NT, heads, hf])
                g.tensor_tensor(rv(0), x1, cs, ALU.mult)
                g.tensor_tensor(rv(1), x2, sn, ALU.mult)
                g.tensor_tensor(rv(2), x2, cs, ALU.mult)
                link(g.tensor_tensor(rv(3), x1, sn, ALU.mult))
                g.tensor_tensor(x1, rv(0), rv(1), ALU.subtract)
                return g.tensor_tensor(x2, rv(2), rv(3), ALU.add)

            def heads_view(t, n):
                return t.rearrange("p t (h d) -> p t h d", h=n)

            def frac_batch(l, b):
                upto = counter(l)
                if b == 0:
                    pool.wait_ge(s5_phase, upto(s5_phase, 1))
                    if l == 0:
                        pool.wait_ge(used, upto(used, 0))
                    else:
                        pool.wait_ge(stepped, counter(l - 1)(stepped, NUM["glu1"] + 1))
                h_ = tab[:, b % 2]
                for jj in range(TB):
                    ins = g.tensor_scalar(h_[:, 0, jj, :], tvec[:], s5[:, 4, TB * b + jj:TB * b + jj + 1], None, ALU.mult)
                link(ins)
                link(g.tensor_scalar(h_[:, 1], h_[:, 0], MAGIC, None, ALU.add))
                link(g.tensor_scalar(h_[:, 1], h_[:, 1], MAGIC, None, ALU.subtract))
                link(g.tensor_tensor(h_[:, 0], h_[:, 0], h_[:, 1], ALU.subtract))
                link(g.tensor_scalar(h_[:, 1], h_[:, 0], 0.25, None, ALU.is_gt))
                link(g.tensor_tensor(h_[:, 1], h_[:, 0], h_[:, 1], ALU.subtract))
                g.tensor_scalar(h_[:, 1], h_[:, 1], 0.25, None, ALU.add).then_inc(frac, 1)

            def unrotate(l, j):
                upto = counter(l)
                pool.wait_ge(scanned, upto(scanned, j + 1))
                if j >= 2:
                    pool.wait_ge(yprod, upto(yprod, j - 1))
                b, jj = divmod(j, TB)
                z = vz[:, j % 2]
                for i in (1, 0):
                    ins = g.tensor_tensor(qq[:, i], z, tab[:, b % 2, i, jj, :].unsqueeze(1).to_broadcast([P, 2, S]),
                                          ALU.mult)
                link(ins)
                g.tensor_tensor(xs[:, j % 2, 0], qq[:, 1, 0], qq[:, 0, 1], ALU.subtract)
                g.tensor_tensor(xs[:, j % 2, 1], qq[:, 0, 0], qq[:, 1, 1], ALU.add).then_inc(unrot, 1)
                pool.wait_ge(unrot, ST * l + j + 1)

            def head_norm(l, n, v):
                upto = counter(l)
                pool.wait_ge(sq_read, upto(sq_read, n + 1))
                link(rstd(r8[:], sq8[:], HD, 8))
                vv = v.rearrange("p t (h d) -> p (t h) d", d=HD)
                return g.tensor_tensor(vv, vv, r8[:].unsqueeze(2).to_broadcast([P, 8, HD]), ALU.mult)

            for l in range(L):
                upto = counter(l)
                for s in range(SLOTS):
                    if s == 3:
                        pool.wait_ge(rs_sum, upto(rs_sum, 1))
                        link(rstd(rs[:], rs[:], D, 2))
                        g.tensor_scalar(rsh[:], rs[:], 0.5, None, ALU.mult).then_inc(rs_done, 1)
                    if s in (8, 16):
                        i = s // 8 - 1
                        pool.wait_ge(taken, upto(taken, i + 1))
                        if l == 0:
                            pool.wait_ge(rope_ready, counter(None)(rope_ready, 1))
                        rope(heads_view(iq[:, :, i * 512:(i + 1) * 512], 8), 0, 8, 8, 0, True).then_inc(roped_iq, 1)
                        pool.wait_ge(roped_iq, upto(roped_iq, i + 1))
                        frac_batch(l, i)
                    if s == 24:
                        pool.wait_ge(taken, upto(taken, G_MISC + 1))
                        ik = misc[:, :, MISC["ik"]:MISC["ik"] + ID]
                        link(rope(heads_view(ik, 1), 0, 1, 8, 0, True))
                        for i in range(2):
                            g.tensor_copy(ikd[:, :, i * ID:(i + 1) * ID], ik)
                        iw = misc[:, :, MISC["iw"]:MISC["iw"] + IH]
                        link(g.tensor_scalar(iw, iw, IH ** -0.5 * ID ** -0.5, None, ALU.mult))
                        pool.wait_ge(k_sum, upto(k_sum, 1))
                        link(rstd(rk[:], sqk[:], HD, 2))
                        k = misc[:, :, 0:HD]
                        link(g.tensor_tensor(k, k, rk[:].unsqueeze(2).to_broadcast([P, NT, HD]), ALU.mult))
                        kg = pa[:, PC["kg"]:PC["kg"] + HD].unsqueeze(1).to_broadcast([P, NT, HD])
                        link(g.tensor_tensor(k, k, kg, ALU.mult))
                        rope(heads_view(k, 1), 0, 1, 16, 8, True).then_inc(roped_k, 1)
                        pool.wait_ge(roped_k, upto(roped_k, 1))
                    if s == 41:
                        head_norm(l, SQ_DQ, E1[:]).then_inc(normr, 1)
                        pool.wait_ge(normr, upto(normr, 1))
                        qv = E1[:].rearrange("p t (h d) -> p (t h) d", d=HD)
                        qg = pa[:, PC["qg"]:PC["qg"] + HD].unsqueeze(1).to_broadcast([P, 8, HD])
                        link(g.tensor_tensor(qv, qv, qg, ALU.mult))
                        rope(heads_view(E1[:], H), 0, H, 16, 8, True).then_inc(roped_q, 1)
                        pool.wait_ge(roped_q, upto(roped_q, 1))
                    if s - 1 in BU:
                        j = BU[s - 1]
                        unrotate(l, j)
                        if j % TB == TB - 1 and j // TB + 2 < ST // TB:
                            frac_batch(l, j // TB + 2)
                    for at_, n, v in ((64, SQ_DSA, obuf[:, B_DSA]), (66, SQ_MQ, E2[:]), (76, SQ_GLA, obuf[:, B_GLA]),
                                      (91, SQ_MEM, obuf[:, B_MEM]), (93, SQ_S5, obuf[:, B_S5])):
                        if s == at_:
                            head_norm(l, n, v).then_inc(normr, 1)
                            pool.wait_ge(normr, upto(normr, n + 1))

        @block.tensor
        def _(pe):
            mm = nc.tensor.matmul
            plink = linker(pe, pe_own)
            tr = nc.tensor.transpose

            def slot_products(n, l, g, c, hi, lo, width):
                upto = counter(l)
                pe.wait_ge(lo_done, upto(lo_done, n + 1))
                for kk in range(CK):
                    k = CK * c + kk
                    for t in range(NT):
                        o = acc[g % 2][t][:, 0:width]
                        h_, l_ = hi[:, k, t * P:(t + 1) * P], lo[:, k, t * P:(t + 1) * P]
                        wh = whi[:, n % RING, kk * W:kk * W + width]
                        wl = wlo[:, n % RING, kk * W:kk * W + width]
                        mm(o, h_, wh, start=(k == 0), stop=False)
                        mm(o, h_, wl, start=False, stop=False)
                        last = mm(o, l_, wh, start=False, stop=(k == KT - 1))
                last.then_inc(used, 1)

            def turn(l, index, src, c):
                upto = counter(l)
                if l is not None or index >= 1:
                    pe.wait_ge(freeB, upto(freeB, index))
                for kk in range(CK):
                    for t in range(NT):
                        last = tr(bankB[:, (kk * NT + t) * P:(kk * NT + t + 1) * P],
                                  src[:, t, kk * P:(kk + 1) * P], ident[:])
                last.then_inc(wroteB, 1)

            upto = counter(None)
            pe.wait_ge(consts, upto(consts, 1))
            pe.wait_ge(mem_in, upto(mem_in, 16))
            for c in range(NC):
                turn(None, c, memr[:, :, c * 256:(c + 1) * 256], c)
            for n in range(PRO):
                g, c = divmod(n, NC)
                if 4 <= n < 12:
                    turn(None, 8 + n - 4, memr[:, :, (n - 4) * 256:(n - 3) * 256], n - 4)
                if n in TURN_P:
                    i = TURN_P[n]
                    pe.wait_ge(x_in, upto(x_in, 48))
                    turn(None, 16 + i, xr[:, i // 2, :, (i % 2) * 256:(i % 2 + 1) * 256], i)
                if n in (12, 28):
                    ml = n // 16
                    for i in range(2):
                        k = 2 * ml + i
                        if ml >= 1:
                            pe.wait_ge(freeA[i], upto(freeA[i], k // 2))
                        pe.wait_ge(kv_norm, upto(kv_norm, ml + 1))
                        for hh in range(2):
                            for t in range(NT):
                                last = tr(bankA[i][:, (hh * NT + t) * P:(hh * NT + t + 1) * P],
                                          R2[:].rearrange("p a b -> p (a b)").rearrange("p (t d) -> p t d", t=NT)[
                                              :, t, (2 * i + hh) * P:(2 * i + hh + 1) * P], ident[:])
                        last.then_inc(stepped, 1)
                if c == 0 and g >= 2:
                    pe.wait_ge(taken, upto(taken, g - 1))
                if g == 0:
                    pe.wait_ge(freeB, upto(freeB, c + 1))
                if g == 2:
                    pe.wait_ge(freeB, upto(freeB, 8 + c + 1))
                hi, lo = (hhi, hlo) if g < 2 else (mhi, mlo)
                slot_products(n, None, g, c, hi, lo, W)

            def step(l, name):
                upto = counter(l)
                n = NUM[name]
                b = bank_of(name)
                pe.wait_ge(freeA[n % 2], upto(freeA[n % 2], n // 2))

                def q(i, w=P):
                    return b[:, i * w:(i + 1) * w]

                def tok(t):
                    return slice(t * P, (t + 1) * P)
                if name in ("iqT0", "iqT1", "iqT2", "iqT3"):
                    i = int(name[-1])
                    pe.wait_ge(roped_iq, upto(roped_iq, i // 2 + 1))
                    for pp in range(2):
                        for t in range(NT):
                            last = tr(q(pp * NT + t), iq[:, t, (2 * i + pp) * P:(2 * i + pp + 1) * P], ident[:])
                elif name == "ikT":
                    pe.wait_ge(roped_k, upto(roped_k, 1))
                    for t in range(NT):
                        tr(q(t), ikd[:, t, :], ident[:])
                    for t in range(NT):
                        last = tr(q(2 + t), misc[:, t, 0:HD], ident[:])
                elif name == "glrT":
                    for t in range(NT):
                        last = tr(b[0:16, tok(t)], misc[:, t, MISC["glr"]:MISC["glr"] + 16], ident[:])
                elif name == "gate":
                    pe.wait_ge(*result(upto, "glrT"))
                    pe.wait_ge(par_in, upto(par_in, 64))
                    for t in range(NT):
                        last = mm(q(t, S), t1[0:16, 0, tok(t)], wu[:], start=True, stop=True)
                elif name in ("uT0", "uT1"):
                    i = int(name[-1])
                    pe.wait_ge(taken, upto(taken, G_SU + 1))
                    for cc in range(2):
                        for t in range(NT):
                            last = tr(q(cc * NT + t), E1[:, t, (2 * i + cc) * P:(2 * i + cc + 1) * P], ident[:])
                elif name.startswith("rel1"):
                    i = int(name[-1])
                    pe.wait_ge(*result(upto, "iqT3"))
                    pe.wait_ge(*result(upto, "ikT"))
                    r = slice(ID * (i % 2), ID * (i % 2) + ID)
                    for hh in range(2):
                        last = mm(q(hh, S), iqT[r, i // 2 * 2 + hh, P:S], kkT[r, 0, :], start=True, stop=True)
                elif name.startswith("rel0"):
                    i = int(name[-1])
                    r = slice(ID * (i % 2), ID * (i % 2) + ID)
                    for hh in range(4):
                        last = mm(q(hh), iqT[r, i // 2 * 4 + hh, 0:P], kkT[r, 0, 0:P], start=True, stop=True)
                elif name in ("qT0", "qT1"):
                    i = int(name[-1])
                    pe.wait_ge(roped_q, upto(roped_q, 1))
                    for hh in range(2):
                        for t in range(NT):
                            last = tr(q(hh * NT + t), E1[:, t, (2 * i + hh) * P:(2 * i + hh + 1) * P], ident[:])
                elif name.startswith("lg1"):
                    i = int(name[-1])
                    pe.wait_ge(*result(upto, "qT0"))
                    pe.wait_ge(*result(upto, "qT1"))
                    for hh in range(2):
                        last = mm(q(hh, S), qT[:, 2 * i + hh, P:S], kkT[:, 1, :], start=True, stop=True)
                elif name == "lg0":
                    for hh in range(H):
                        last = mm(q(hh), qT[:, hh, 0:P], kkT[:, 1, 0:P], start=True, stop=True)
                elif name in ("cumD", "cumT", "cumL"):
                    pe.wait_ge(lsum, upto(lsum, 1))
                    m = {"cumD": triM, "cumT": tri, "cumL": triL}[name]
                    for t in range(NT):
                        last = mm(q(t, S), m[:], la[:, t, :], start=True, stop=True)
                elif name == "dec":
                    for hp in range(2):
                        for t in range(NT):
                            last = mm(b[:, hp * 4 + t * 2:hp * 4 + t * 2 + 2], la[:, t, hp * P:(hp + 1) * P], cind[:],
                                      start=True, stop=True)
                elif name.startswith("pT1"):
                    i = int(name[-1])
                    pe.wait_ge(exp1, upto(exp1, 1))
                    for hh in range(2):
                        for t in range(NT):
                            last = tr(q(hh * NT + t), P1[:, 2 * i + hh, tok(t)], ident[:])
                elif name == "pT0":
                    pe.wait_ge(exp0, upto(exp0, 1))
                    for hh in range(H):
                        last = tr(q(hh), P0[:, hh, :], ident[:])
                elif name == "pv1":
                    pe.wait_ge(*result(upto, "pT1_0"))
                    pe.wait_ge(*result(upto, "pT1_1"))
                    for hh in range(H):
                        for t in range(NT):
                            last = mm(q(hh), pT[:, hh, t, :], misc[:, t, HD:2 * HD], start=(t == 0), stop=(t == 1))
                elif name == "pv0":
                    pe.wait_ge(*result(upto, "pT0"))
                    for hh in range(H):
                        last = mm(q(hh), pT[:, hh, 0, :], misc[:, 0, HD:2 * HD], start=True, stop=True)
                elif name in ("qeT", "keT", "qbT"):
                    src = {"qeT": t1, "keT": t2, "qbT": t3}[name]
                    pe.wait_ge(gmul, upto(gmul, {"qeT": 1, "keT": 1, "qbT": 2}[name]))
                    for hp in range(2):
                        for t in range(NT):
                            last = tr(q(hp * NT + t), src[:, t, hp * P:(hp + 1) * P], ident[:])
                elif name in ("at0", "at1"):
                    t = int(name[-1])
                    pe.wait_ge(*result(upto, "qeT"))
                    pe.wait_ge(*result(upto, "keT"))
                    for hh in (0, 2, 1, 3):
                        r = slice(GD * (hh % 2), GD * (hh % 2) + GD)
                        last = mm(q(hh), keT[r, hh // 2, tok(t)], qeT[r, hh // 2, tok(t)], start=True, stop=True)
                        if hh == 2:
                            plink(last)
                elif name in ("dS0", "dS1"):
                    pe.wait_ge(gmul, upto(gmul, 3))
                    pe.wait_ge(taken, upto(taken, G_GV + 1))
                    for i, ch in enumerate((0, 1) if name == "dS0" else (2,)):
                        r = slice(GD * (ch % 2), GD * (ch % 2) + GD)
                        for hh in range(H):
                            o = b[GD * (hh % 2):GD * (hh % 2) + GD, (2 * i + hh // 2) * P:(2 * i + hh // 2 + 1) * P]
                            last = mm(o, kd[r, ch // 2, hh * GD:(hh + 1) * GD], E1[r, ch // 2, hh * P:(hh + 1) * P],
                                      start=True, stop=True)
                        if ch == 0:
                            plink(last)
                elif name in ("go0", "go1"):
                    t = int(name[-1])
                    pe.wait_ge(*result(upto, f"at{t}"))
                    pe.wait_ge(*result(upto, "dS0"))
                    pe.wait_ge(*result(upto, "dS1"))
                    pe.wait_ge(*result(upto, "qbT"))
                    for hh in range(H):
                        last = mm(q(hh), attn[:, hh, :], E1[:, t, hh * P:(hh + 1) * P], start=(hh == 0),
                                  stop=False, skip_group_check=True)
                    plink(last)
                    for hh in (0, 2, 1, 3):
                        r = slice(GD * (hh % 2), GD * (hh % 2) + GD)
                        for cc in range(2):
                            ch = 2 * t + cc
                            if ch > 0:
                                last = mm(b[GD * cc:GD * cc + GD, hh * P:(hh + 1) * P],
                                          qbT[r, hh // 2, ch * GD:(ch + 1) * GD], stt_[r, ch - 1, hh // 2, :],
                                          start=False, stop=True, skip_group_check=True)
                        if hh == 2:
                            plink(last)
                elif name in ("mqT0", "mqT1"):
                    i = int(name[-1])
                    pe.wait_ge(normr, upto(normr, SQ_MQ + 1))
                    for hh in range(2):
                        for t in range(NT):
                            last = tr(q(hh * NT + t), E2[:, t, (2 * i + hh) * P:(2 * i + hh + 1) * P], ident[:])
                elif name[:2] == "ml":
                    t, i = int(name[2]), int(name[4])
                    pe.wait_ge(*result(upto, "mqT0"))
                    pe.wait_ge(*result(upto, "mqT1"))
                    pe.wait_ge(mk_in, upto(mk_in, 16))
                    for hh in range(2):
                        last = mm(q(hh, S), mqT[:, 2 * i + hh, tok(t)], mkT[:, 2 * i + hh, :], start=True, stop=True)
                elif name[:2] == "mp":
                    t, i = int(name[2]), int(name[4])
                    pe.wait_ge(*result(upto, f"ml{t}_0"))
                    pe.wait_ge(*result(upto, f"ml{t}_1"))
                    for hh in range(2):
                        for st in range(NT):
                            last = tr(q(hh * NT + st), Pm[:, 2 * i + hh, tok(st)], ident[:])
                elif name[:2] == "mv":
                    t = int(name[2])
                    pe.wait_ge(*result(upto, f"mp{t}_0"))
                    pe.wait_ge(*result(upto, f"mp{t}_1"))
                    pe.wait_ge(mv_in, upto(mv_in, 16))
                    for hh in range(H):
                        for st in range(NT):
                            last = mm(q(hh), pT[:, hh, st, :], mv[:, st, hh * P:(hh + 1) * P],
                                      start=(st == 0), stop=(st == 1))
                elif name[:2] == "yt":
                    t = int(name[2])
                    pe.wait_ge(gelud, upto(gelud, 4))
                    for ct in range(4):
                        last = tr(q(ct), ych[:, ct, tok(t)], ident[:])
                elif name[:3] == "glu":
                    t = int(name[3])
                    pe.wait_ge(glu_in, upto(glu_in, 16))
                    for ct in range(4):
                        last = mm(b[:], ych[:, ct, tok(t)], wg[:, ct, :], start=(ct == 0), stop=(ct == 3))
                last.then_inc(stepped, 1)

            for l in range(L):
                upto = counter(l)
                for s in range(SLOTS):
                    g, c = divmod(s, NC)
                    if s in AT:
                        step(l, AT[s])
                    if s in TURN_X:
                        if l == 0:
                            pe.wait_ge(x_in, upto(x_in, 0))
                        else:
                            pe.wait_ge(added, upto(added, 0))
                        cx = TURN_X[s]
                        turn(l, BX + s - 2, xr[:, 0, :, (cx % 2) * 256:(cx % 2 + 1) * 256], cx)
                    if s in BU:
                        j = BU[s]
                        ct, jj = divmod(j, 4)
                        pe.wait_ge(freeB, upto(freeB, BBU + j))
                        if j == 0:
                            pe.wait_ge(par_in, upto(par_in, 64))
                            pe.wait_ge(*result(upto, "uT0"))
                            pe.wait_ge(*result(upto, "uT1"))
                        r = slice(32 * jj, 32 * jj + 32)
                        for i in range(2):
                            last = mm(bankB[:, i * S:(i + 1) * S], bm[r, ct, i, :], uT[r, ct, :], start=True, stop=True)
                        last.then_inc(wroteB, 1)
                    if s in YS:
                        j = YS[s]
                        ct, jj = divmod(j, 4)
                        pe.wait_ge(unrot, upto(unrot, j + 1))
                        if j == 0:
                            pe.wait_ge(s5_c, upto(s5_c, 1))
                        if jj == 0 and l + ct >= 1:
                            pe.wait_ge(ypoly, upto(ypoly, ct))
                        r = slice(32 * jj, 32 * jj + 32)
                        o = bankY[r, ct % 2, :]
                        mm(o, cp[:, j, 0, :], xs[:, j % 2, 0], start=True, stop=False, skip_group_check=True)
                        mm(o, cp[:, j, 1, :], xs[:, j % 2, 1], start=False, stop=True,
                           skip_group_check=True).then_inc(yprod, 1)
                    if s in TURN_O:
                        co = TURN_O[s]
                        pe.wait_ge(zmul, upto(zmul, co // 2 + 1))
                        turn(l, BO + co, obuf[:, co // 2, :, (co % 2) * 256:(co % 2 + 1) * 256], co)
                    if s in TURN_N and l + 1 < L:
                        cn = TURN_N[s]
                        pe.wait_ge(added, upto(added, cn // 2 + 1))
                        turn(l, BN + cn, xr[:, cn // 2, :, (cn % 2) * 256:(cn % 2 + 1) * 256], cn)
                    if c == 0:
                        if g < 2:
                            if l == 0:
                                pe.wait_ge(taken, upto(taken, g - 1))
                            else:
                                pe.wait_ge(added, upto(added, g - 1))
                        elif g - 2 < 8:
                            pe.wait_ge(taken, upto(taken, g - 1))
                        elif g - 2 < 12:
                            pe.wait_ge(gated, upto(gated, g - 2 - 8 + 1))
                        else:
                            pe.wait_ge(added, upto(added, g - 2 - 12 + 1))
                    if g == 0:
                        if c < 6:
                            pe.wait_ge(freeB, upto(freeB, c - 6 + 1))
                        else:
                            pe.wait_ge(freeB, upto(freeB, BX + c - 6 + 1))
                    if g == G_OUT:
                        pe.wait_ge(freeB, upto(freeB, BO + c + 1))
                    slot_products(s, l, g, c, hhi, hlo, MISC["end"] if g == G_MISC else W)

        @block.scalar
        def _(act):
            link = linker(act, act_own)
            fn = nc.scalar.activation
            R2f = R2[:].rearrange("p a b -> p (a b)")

            def split_hi(n, l):
                upto = counter(l)
                act.wait_ge(landed[n % RING], upto(landed[n % RING], 16 * (n // RING + 1)))
                if l is not None or n >= RING:
                    act.wait_ge(used, upto(used, n - RING + 1))
                fn(whi[:, n % RING, :], raw[:, n % RING, :], ACT.Copy).then_inc(hi_done, 1)

            def turn_hi(l, index, dst, gain, c, free_at):
                upto = counter(l)
                act.wait_ge(wroteB, upto(wroteB, index + 1))
                if free_at is not None:
                    act.wait_ge(used, upto(used, free_at))
                for kk in range(CK):
                    k = CK * c + kk
                    ins = fn(dst[:, k, :], bankB[:, kk * S:(kk + 1) * S], ACT.Copy, scale=gain(k))
                ins.then_inc(turned_hi, 1)

            def square_piece(b, g):
                for t in range(NT):
                    ins = fn(E3[:, t, :], xr[:, b, t, :], ACT.Square, accum_out=ssx[:, t, g:g + 1])
                ins.then_inc(sq_x, 1)

            def copy(name, dst, **kw):
                fn(dst, bank_of(name)[:], ACT.Copy, **kw).then_inc(freeA[NUM[name] % 2], 1)

            upto = counter(None)
            act.wait_ge(mem_in, upto(mem_in, 16))
            for t in range(NT):
                for i in range(4):
                    link(fn(R2f[:, 0:W], memr[:, t, i * W:(i + 1) * W], ACT.Square, accum_out=ssm[:, t, i:i + 1]))
            fn(R2f[:, 0:8], ssm[:].rearrange("p a b -> p (a b)"), ACT.Copy).then_inc(sq_mem, 1)
            act.wait_ge(const_in, upto(const_in, 48))
            for n in range(AHEAD):
                split_hi(n, None)
            for c in range(NC):
                turn_hi(None, c, hhi, lambda k: mg[:, 0, k:k + 1], c, None)
            for n in range(PRO):
                if n + AHEAD < PRO:
                    split_hi(n + AHEAD, None)
                else:
                    split_hi(n + AHEAD - PRO, 0)
                if 4 <= n < 12:
                    turn_hi(None, 8 + n - 4, mhi, lambda k: mg[:, 1, k:k + 1], n - 4, None)
                if n in TURN_P:
                    if n == 20:
                        act.wait_ge(par_in, upto(par_in, 64))
                    turn_hi(None, 16 + TURN_P[n], hhi, lambda k: col("ln", k), TURN_P[n], NC + TURN_P[n] + 1)
                if n == 5:
                    act.wait_ge(ang_ready, upto(ang_ready, 1))
                    for i in range(2):
                        ins = fn(snc[:, i], ang[:, i], ACT.Sin)
                    ins.then_inc(rope_ready, 1)
                if n in (8, 24):
                    ml = n // 16
                    act.wait_ge(used, upto(used, n))
                    act.wait_ge(rm_done, upto(rm_done, 1))
                    if ml == 1:
                        act.wait_ge(k_out[0], 16)
                    for t in range(NT):
                        ins = fn(R2f[:, t * W:(t + 1) * W], acc[0][t][:], ACT.Copy, scale=rm[:, t:t + 1])
                    ins.then_inc(taken, 1)
                    act.wait_ge(taken, upto(taken, 2 * ml + 1))
                    fn(kvT[:].rearrange("p a b -> p (a b)"), R2f, ACT.Square).then_inc(sq_kv, 1)
                if n in (13, 29):
                    ml = n // 16
                    for i in range(2):
                        act.wait_ge(stepped, upto(stepped, 2 * ml + 2))
                        fn(kvT[:, 2 * i:2 * i + 2, :].rearrange("p a b -> p (a b)"), bankA[i][:], ACT.Copy,
                           scale=mg[:, ml, MG["mk"]:MG["mk"] + 1]).then_inc(freeA[i], 1)
                if n == 16:
                    act.wait_ge(used, upto(used, 16))
                    for t in range(NT):
                        ins = fn(R1[:, t, :], acc[1][t][:], ACT.Copy, scale=rm[:, t:t + 1])
                    ins.then_inc(taken, 1)
                if n in (21, 23, 27):
                    if n == 21:
                        act.wait_ge(x_in, upto(x_in, 48))
                    i = {21: 0, 23: 1, 27: 2}[n]
                    square_piece(i, i)

            dst_of = {G_IQ0: iq[:, :, 0:W], G_IQ1: iq[:, :, W:2 * W], G_MISC: misc[:], G_SU: E1[:], G_DQ: E1[:],
                      G_GQK: E2[:], G_GV: E1[:], G_MQ: E2[:]}
            for l in range(L):
                upto = counter(l)
                for s in range(SLOTS):
                    g, c = divmod(s, NC)
                    if s + AHEAD < SLOTS:
                        split_hi(s + AHEAD, l)
                    elif l + 1 < L:
                        split_hi(s + AHEAD - SLOTS, l + 1)
                    if s in TURN_X:
                        cx = TURN_X[s]
                        turn_hi(l, BX + s - 2, hhi, lambda k: col("ln", k), cx,
                                NC + cx + 1 - PRO if l == 0 else (GROUPS - 1) * NC + cx + 1 - SLOTS)
                    if s in TURN_O:
                        co = TURN_O[s]
                        turn_hi(l, BO + co, hhi, lambda k: col("on", k), co, (G_OUT - 1) * NC + co + 1)
                    if s in TURN_N and l + 1 < L:
                        cn = TURN_N[s]
                        act.wait_ge(par_in, upto(par_in, 128))
                        turn_hi(l, BN + cn, hhi, lambda k: col("ln", k), cn, (GROUPS - 1) * NC + cn + 1)
                    if s == 0 and l == 0:
                        act.wait_ge(used, counter(None)(used, PRO))
                        act.wait_ge(v_out[0], 16)
                        for t in range(NT):
                            ins = fn(R1[:, t, :], acc[1][t][:], ACT.Copy, scale=rm[:, t:t + 1])
                        ins.then_inc(taken, 1)
                    if s == 1:
                        if l == 0:
                            act.wait_ge(x_in, upto(x_in, 0))
                        else:
                            act.wait_ge(added, upto(added, 0))
                        square_piece(0, 3)
                    if s == 2:
                        if l == 0:
                            act.wait_ge(par_in, counter(l)(par_in, 64))
                        fn(s5[:, 0, :], pa[:, PC["lst"]:PC["lst"] + ST], ACT.Exp).then_inc(s5_exp, 1)
                    if s == 5:
                        act.wait_ge(s5_phase, upto(s5_phase, 1))
                        fn(s5[:, 5, :], s5[:, 1, :], ACT.Exp)
                        fn(s5[:, 6, :], s5[:, 4, :], ACT.Sin, scale=3.1415925)
                        fn(s5[:, 7, :], s5[:, 4, :], ACT.Sin, scale=6.283185).then_inc(s5_sin, 1)
                    if s in (17, 26, 49, 59):
                        b = (17, 26, 49, 59).index(s)
                        act.wait_ge(frac, upto(frac, b + 1))
                        v = tab[:, b % 2].rearrange("p a j s -> p (a j s)")
                        fn(v, v, ACT.Sin, scale=6.283185).then_inc(phased, 1)
                    if c == 0 and 1 <= g <= 8:
                        act.wait_ge(used, upto(used, NC * g))
                        if g == 1:
                            act.wait_ge(rs_done, upto(rs_done, 1))
                            if l == 0:
                                act.wait_ge(used, counter(None)(used, PRO))
                            else:
                                act.wait_ge(freeB, counter(l - 1)(freeB, BO + 8))
                        if g - 1 == G_DQ:
                            act.wait_ge(stepped, upto(stepped, NUM["uT1"] + 1))
                        if g - 1 == G_GV:
                            act.wait_ge(stepped, upto(stepped, NUM["qT1"] + 1))
                        if g - 1 == G_MQ:
                            act.wait_ge(gmul, upto(gmul, 3))
                        w = MISC["end"] if g - 1 == G_MISC else W
                        for t in range(NT):
                            ins = fn(dst_of[g - 1][:, t, :], acc[(g - 1) % 2][t][:, 0:w], ACT.Copy,
                                     scale=rs[:, t:t + 1])
                        ins.then_inc(taken, 1)
                    if c == 0 and 9 <= g <= 12:
                        z = g - 9
                        act.wait_ge(used, upto(used, NC * g))
                        if l + z >= 1:
                            act.wait_ge(zmul, upto(zmul, z))
                        if z == 0:
                            act.wait_ge(stepped, upto(stepped, NUM["dec"] + 1))
                        for t in range(NT):
                            ins = fn(Ez[:, t, :], acc[(g - 1) % 2][t][:], ACT.Tanh, scale=rsh[:, t:t + 1])
                        ins.then_inc(ztanh, 1)
                    if s in (105, 113, 121) and l + 1 < L:
                        g_ = (s - 105) // 8
                        act.wait_ge(added, upto(added, g_ + 1))
                        square_piece(g_, g_)
                    for n, (at_, src) in enumerate(((41, E1), (64, None), (66, E2), (76, None), (91, None), (93, None))):
                        if s != at_:
                            continue
                        if l + n >= 1:
                            act.wait_ge(sq_read, upto(sq_read, n))
                        if n == SQ_DQ:
                            act.wait_ge(taken, upto(taken, G_DQ + 1))
                        if n == SQ_MQ:
                            act.wait_ge(taken, upto(taken, G_MQ + 1))
                        if n == SQ_DSA:
                            act.wait_ge(*result(upto, "pv1"))
                            act.wait_ge(*result(upto, "pv0"))
                        if n == SQ_GLA:
                            act.wait_ge(*result(upto, "go1"))
                        if n == SQ_MEM:
                            act.wait_ge(*result(upto, "mv0"))
                            act.wait_ge(*result(upto, "mv1"))
                        if n == SQ_S5:
                            act.wait_ge(obr, upto(obr, 1))
                        b = {SQ_DSA: B_DSA, SQ_GLA: B_GLA, SQ_MEM: B_MEM, SQ_S5: B_S5}.get(n)
                        v = src[:] if src is not None else obuf[:, b]
                        fn(E3[:], v, ACT.Square).then_inc(squared, 1)
                    if s in AT:
                        name = AT[s]
                        n = NUM[name]
                        b = bank_of(name)
                        fa = freeA[n % 2]
                        if name not in ("gate", "lg1_0", "lg1_1", "lg0", "pv1", "pv0", "at0", "at1", "dS0", "dS1",
                                        "go0", "go1", "mv0", "mv1"):
                            act.wait_ge(stepped, upto(stepped, n + 1))
                        if name[:3] == "iqT":
                            i = int(name[-1])
                            copy(name, iqT[:, 2 * i:2 * i + 2, :].rearrange("p a b -> p (a b)"))
                        elif name == "ikT":
                            copy(name, kkT[:].rearrange("p a b -> p (a b)"))
                        elif name == "glrT":
                            fn(t1[0:16, 0, :], b[0:16, 0:S], ACT.Copy).then_inc(fa, 1)
                        elif name in ("uT0", "uT1"):
                            i = int(name[-1])
                            copy(name, uT[:, 2 * i:2 * i + 2, :].rearrange("p a b -> p (a b)"))
                        elif name[:3] == "rel":
                            i = n - NUM["rel1_0"]
                            if l == 0 and i == 0:
                                act.wait_ge(v_out[1], 16)
                            if i >= 2:
                                act.wait_ge(weighed, upto(weighed, i - 1))
                            fn(rel[:, i % 2, :], b[:], ACT.Relu).then_inc(fa, 1)
                        elif name in ("qT0", "qT1"):
                            i = int(name[-1])
                            copy(name, qT[:, 2 * i:2 * i + 2, :].rearrange("p a b -> p (a b)"))
                        elif name == "cumD":
                            bb = b[:].rearrange("p (t d) -> p t d", t=NT)
                            fn(t1[:], bb, ACT.Exp, scale=1.0 / 16)
                            fn(t2[:], bb, ACT.Exp, scale=-1.0 / 16).then_inc(fa, 1)
                        elif name in ("cumT", "cumL"):
                            fn((t3 if name == "cumT" else kd)[:], b[:].rearrange("p (t d) -> p t d", t=NT), ACT.Exp,
                               scale=1.0 / 16).then_inc(fa, 1)
                        elif name == "dec":
                            fn(dec[:], b[:, 0:8].rearrange("p (a c) -> p a c", a=2), ACT.Exp, scale=1.0 / 16).then_inc(fa, 1)
                        elif name[:3] == "pT1":
                            i = int(name[-1])
                            copy(name, pT[:, 2 * i:2 * i + 2].rearrange("p a b c -> p (a b c)"))
                        elif name == "pT0":
                            act.wait_ge(stepped, upto(stepped, NUM["pv1"] + 1))
                            fn(pT[:, :, 0, :], b[:].rearrange("p (h t) -> p h t", h=H), ACT.Copy).then_inc(fa, 1)
                        elif name in ("qeT", "keT", "qbT"):
                            copy(name, {"qeT": qeT, "keT": keT, "qbT": qbT}[name][:].rearrange("p a b -> p (a b)"))
                        elif name in ("mqT0", "mqT1"):
                            i = int(name[-1])
                            copy(name, mqT[:, 2 * i:2 * i + 2, :].rearrange("p a b -> p (a b)"), scale=col("mqg"))
                        elif name[:2] == "ml":
                            t, i = int(name[2]), int(name[4])
                            act.wait_ge(mmax, upto(mmax, 2 * t + i + 1))
                            if t == 1 and i == 0:
                                act.wait_ge(stepped, upto(stepped, NUM["mp0_1"] + 1))
                            for hh in range(2):
                                h_ = 2 * i + hh
                                ins = fn(Pm[:, h_, :], b[:, hh * S:(hh + 1) * S], ACT.Exp, scale=SCALE,
                                         bias=(nm0, nm1)[t][:, h_:h_ + 1], accum_out=(su0, su1)[t][:, h_:h_ + 1])
                            ins.then_inc(fa, 1)
                        elif name[:2] == "mp":
                            t, i = int(name[2]), int(name[4])
                            if t == 1 and i == 0:
                                act.wait_ge(stepped, upto(stepped, NUM["mv0"] + 1))
                            copy(name, pT[:, 2 * i:2 * i + 2].rearrange("p a b c -> p (a b c)"))
                        elif name[:2] == "yt":
                            t = int(name[2])
                            copy(name, obuf[:, B_S5, t, :])
                        elif name[:3] == "glu":
                            copy_ = fn(gt[:, int(name[3]), :], b[:], ACT.Tanh, scale=0.5)
                            copy_.then_inc(fa, 1)
                    if s == 33:
                        act.wait_ge(*result(upto, "gate"))
                        link(fn(t1[:], la[:], ACT.Abs))
                        link(fn(t1[:], t1[:], ACT.Exp, scale=-1.0))
                        fn(t1[:], t1[:], ACT.Ln, bias=1.0).then_inc(lsoft, 1)
                    if s == 54:
                        act.wait_ge(biased1, upto(biased1, 1))
                        for hh in range(H):
                            ins = fn(P1[:, hh, :], P1[:, hh, :], ACT.Exp, bias=nm1[:, hh:hh + 1],
                                     accum_out=su1[:, hh:hh + 1])
                        ins.then_inc(exp1, 1)
                    if s == 57:
                        act.wait_ge(biased0, upto(biased0, 1))
                        for hh in range(H):
                            ins = fn(P0[:, hh, :], P0[:, hh, :], ACT.Exp, bias=nm0[:, hh:hh + 1],
                                     accum_out=su0[:, hh:hh + 1])
                        ins.then_inc(exp0, 1)
                    for ct in range(4):
                        if s == S5_SLOT[4 * ct + 3] + S5_LAG + 2:
                            act.wait_ge(ypoly, upto(ypoly, ct + 1))
                            fn(ytmp[:], ytmp[:], ACT.Tanh, scale=math.sqrt(2 / math.pi)).then_inc(ytanh, 1)

        @block.vector
        def _(dve):
            link = linker(dve, dve_own)
            v_ = nc.vector

            def split_lo(n, l):
                upto = counter(l)
                dve.wait_ge(hi_done, upto(hi_done, n + 1))
                v_.tensor_tensor(wlo[:, n % RING, :], raw[:, n % RING, :], whi[:, n % RING, :].bitcast(F32),
                                 ALU.subtract).then_inc(lo_done, 1)

            def turn_lo(l, index, count, hi, lo, gain, c):
                upto = counter(l)
                dve.wait_ge(turned_hi, upto(turned_hi, count))
                for kk in range(CK):
                    k = CK * c + kk
                    ins = v_.scalar_tensor_tensor(out=lo[:, k, :], in0=bankB[:, kk * S:(kk + 1) * S], scalar=gain(k),
                                                  in1=hi[:, k, :].bitcast(F32), op0=ALU.mult, op1=ALU.subtract)
                ins.then_inc(freeB, 1)

            def x_add(l, g):
                upto = counter(l)
                dve.wait_ge(used, upto(used, (G_OUT + g + 1) * NC))
                dve.wait_ge(x_in, upto(x_in, 48 if g < 3 else 64))
                for t in range(NT):
                    ins = v_.tensor_tensor(xr[:, g % XB, t, :], acc[g % 2][t][:], xr[:, g % XB, t, :], ALU.add)
                ins.then_inc(added, 1)

            def sum8(dst, src, n):
                return v_.tensor_reduce(dst, src, AX.X, ALU.add)

            upto = counter(None)
            dve.wait_ge(sq_mem, upto(sq_mem, 1))
            sum8(rm[:], ssm[:], 2).then_inc(rm_sum, 1)
            for n in range(AHEAD):
                split_lo(n, None)
            for c in range(NC):
                turn_lo(None, c, c + 1, hhi, hlo, lambda k: mg[:, 0, k:k + 1], c)
            for n in range(PRO):
                if n + AHEAD < PRO:
                    split_lo(n + AHEAD, None)
                else:
                    split_lo(n + AHEAD - PRO, 0)
                if 4 <= n < 12:
                    turn_lo(None, 8 + n - 4, 8 + n - 4 + 1, mhi, mlo, lambda k: mg[:, 1, k:k + 1], n - 4)
                if n in TURN_P:
                    i = TURN_P[n]
                    turn_lo(None, 16 + i, 16 + i + 1, hhi, hlo, lambda k: col("ln", k), i)
                if n in (8, 24):
                    ml = n // 16
                    dve.wait_ge(sq_kv, upto(sq_kv, ml + 1))
                    sum8(sq8[:], kvT[:].rearrange("p a b -> p (a b)").rearrange("p (n d) -> p n d", d=HD), 8)\
                        .then_inc(kv_sum, 1)

            rotv = rot[:].rearrange("p a i s -> p a (i s)")
            for l in range(L):
                upto = counter(l)
                s5r = lambda i: s5[:, i, :]

                def topk(score, first, count):
                    for _ in range(count):
                        link(v_.max(mx8[:], score))
                        link(v_.match_replace(score, mx8[:], score, TAKEN))

                def key_bias(dst, score, causal):
                    link(v_.scalar_tensor_tensor(out=dst, in0=score, scalar=0.5 * (NEG + TAKEN), in1=causal,
                                                 op0=ALU.is_le, op1=ALU.mult))
                    link(v_.tensor_scalar(dst, dst, 1.0, BIG, ALU.subtract, ALU.mult))

                for s in range(SLOTS):
                    g, c = divmod(s, NC)
                    if s + AHEAD < SLOTS:
                        split_lo(s + AHEAD, l)
                    elif l + 1 < L:
                        split_lo(s + AHEAD - SLOTS, l + 1)
                    if s == 0 and l > 0:
                        x_add(l - 1, 3)
                    if s in TURN_X:
                        turn_lo(l, BX + s - 2, s - 1, hhi, hlo, lambda k: col("ln", k), TURN_X[s])
                    if s in TURN_O:
                        co = TURN_O[s]
                        turn_lo(l, BO + co, 2 + co + 1, hhi, hlo, lambda k: col("on", k), co)
                    if s in TURN_N and l + 1 < L:
                        cn = TURN_N[s]
                        turn_lo(l, BN + cn, 10 + cn + 1, hhi, hlo, lambda k: col("ln", k), cn)
                    if s == 1:
                        dve.wait_ge(sq_x, upto(sq_x, 1))
                        sum8(rs[:], ssx[:], 2).then_inc(rs_sum, 1)
                    if s == 3:
                        dve.wait_ge(s5_exp, upto(s5_exp, 1))
                        are, aim = pa[:, PC["are"]:PC["are"] + ST], pa[:, PC["aim"]:PC["aim"] + ST]
                        v_.tensor_tensor(s5r(1), are, s5r(0), ALU.mult)
                        link(v_.tensor_tensor(s5r(2), aim, s5r(0), ALU.mult))
                        link(v_.tensor_scalar(s5r(2), s5r(2), 1.0 / TWO_PI, None, ALU.mult))
                        link(v_.tensor_scalar(s5r(3), s5r(2), MAGIC, None, ALU.add))
                        link(v_.tensor_scalar(s5r(3), s5r(3), MAGIC, None, ALU.subtract))
                        v_.tensor_tensor(s5r(4), s5r(2), s5r(3), ALU.subtract).then_inc(s5_phase, 1)
                    if s == 6:
                        dve.wait_ge(s5_sin, upto(s5_sin, 1))
                        if l > 0:
                            dve.wait_ge(x_out, upto(x_out, 0))
                        r_, sh, s1 = s5r(5), s5r(6), s5r(7)
                        link(v_.tensor_tensor(s5r(8), sh, sh, ALU.mult))
                        link(v_.tensor_tensor(s5r(9), r_, s5r(8), ALU.mult))
                        link(v_.tensor_scalar(s5r(10), r_, 1.0, None, ALU.subtract))
                        link(v_.scalar_tensor_tensor(out=s5r(10), in0=s5r(9), scalar=-2.0, in1=s5r(10), op0=ALU.mult,
                                                     op1=ALU.add))
                        v_.tensor_tensor(s5r(11), r_, s1, ALU.mult)
                        v_.tensor_tensor(s5r(8), are, are, ALU.mult)
                        link(v_.tensor_tensor(s5r(9), aim, aim, ALU.mult))
                        link(v_.tensor_tensor(s5r(8), s5r(8), s5r(9), ALU.add))
                        link(v_.reciprocal(s5r(8), s5r(8)))
                        for dst, a0, a1, op in ((12, 10, 11, ALU.add), (13, 11, 10, ALU.subtract)):
                            link(v_.tensor_tensor(s5r(9), s5r(a0), are, ALU.mult))
                            link(v_.tensor_tensor(s5r(14), s5r(a1), aim, ALU.mult))
                            link(v_.tensor_tensor(s5r(9), s5r(9), s5r(14), op))
                            link(v_.tensor_tensor(s5r(dst), s5r(9), s5r(8), ALU.mult))
                        fre, fim = (s5r(i).unsqueeze(2).to_broadcast([P, ST, 32]) for i in (12, 13))
                        tv = [t_[:].rearrange("p t d -> p (t d)").rearrange("p (j c) -> p j c", j=ST)
                              for t_ in (t1, t2, t3, kd)]
                        v_.tensor_tensor(tv[0], cp[:, :, 0, :], fre, ALU.mult)
                        v_.tensor_tensor(tv[1], cp[:, :, 1, :], fim, ALU.mult)
                        v_.tensor_tensor(tv[2], cp[:, :, 0, :], fim, ALU.mult)
                        link(v_.tensor_tensor(tv[3], cp[:, :, 1, :], fre, ALU.mult))
                        v_.tensor_tensor(cp[:, :, 0, :], tv[0], tv[1], ALU.subtract)
                        v_.scalar_tensor_tensor(out=cp[:, :, 1, :], in0=tv[2], scalar=-1.0, in1=tv[3], op0=ALU.mult,
                                                op1=ALU.subtract).then_inc(s5_c, 1)
                        dve.wait_ge(s5_c, upto(s5_c, 1))
                    if s == 24:
                        dve.wait_ge(taken, upto(taken, G_MISC + 1))
                        for t in range(NT):
                            link(v_.tensor_tensor(ytmp[:, t * HD:(t + 1) * HD], misc[:, t, 0:HD], misc[:, t, 0:HD], ALU.mult))
                        sum8(sqk[:], ytmp[:].rearrange("p (t d) -> p t d", t=NT), 2).then_inc(k_sum, 1)
                    if s == SLOT["gate"]:
                        dve.wait_ge(stepped, upto(stepped, NUM["gate"] + 1))
                        bup = pa[:, PC["bup"]:PC["bup"] + S].unsqueeze(1).to_broadcast([P, NT, S])
                        v_.tensor_tensor(la[:], bank_of("gate")[:].rearrange("p (t d) -> p t d", t=NT), bup,
                                         ALU.add).then_inc(freeA[NUM["gate"] % 2], 1)
                    if s == 34:
                        dve.wait_ge(lsoft, upto(lsoft, 1))
                        v_.scalar_tensor_tensor(out=la[:], in0=la[:], scalar=0.0, in1=t1[:], op0=ALU.min,
                                                op1=ALU.subtract).then_inc(lsum, 1)
                    if s in AT and AT[s][:3] == "rel":
                        name = AT[s]
                        i = NUM[name] - NUM["rel1_0"]
                        dve.wait_ge(*result(upto, name))
                        if i == 0:
                            dve.wait_ge(roped_k, upto(roped_k, 1))
                        for hh in range(2 if i < 8 else 4):
                            if i < 8:
                                h_, t, w, dst, z = 2 * (i // 2 * 2 + hh) + i % 2, 1, S, sc[:], negm[:]
                            else:
                                h_, t, w, dst, z = 2 * ((i - 8) // 2 * 4 + hh) + i % 2, 0, P, sc0[:], negm[:, P:S]
                            ins = v_.scalar_tensor_tensor(
                                out=dst, in0=rel[:, i % 2, hh * w:(hh + 1) * w],
                                scalar=misc[:, t, MISC["iw"] + h_:MISC["iw"] + h_ + 1], in1=z if h_ == 0 else dst,
                                op0=ALU.mult, op1=ALU.add)
                            if hh < (1 if i < 8 else 3):
                                link(ins)
                        ins.then_inc(weighed, 1)
                        dve.wait_ge(weighed, upto(weighed, i + 1))
                    if 44 <= s < 48:
                        topk(sc[:], s == 44, 2)
                    if s == 48:
                        key_bias(bias1[:], sc[:], c01[:])
                    if 48 <= s < 52:
                        topk(sc0[:], s == 48, 2)
                    if s == 52:
                        key_bias(bias0[:], sc0[:], c01[:, P:S])
                    if s in (41, 64, 66, 76, 91, 93):
                        n = (41, 64, 66, 76, 91, 93).index(s)
                        dve.wait_ge(squared, upto(squared, n + 1))
                        if l + n >= 1:
                            dve.wait_ge(normr, upto(normr, n))
                        sum8(sq8[:], E3[:].rearrange("p t (h d) -> p (t h) d", d=HD), 8).then_inc(sq_read, 1)
                    if s in AT:
                        name = AT[s]
                        n = NUM[name]
                        b = bank_of(name)
                        fa = freeA[n % 2]
                        b4 = b[:].rearrange("p (h d) -> p h d", h=H)
                        if name in ("lg1_0", "lg1_1", "lg0"):
                            dve.wait_ge(stepped, upto(stepped, n + 1))
                            if name == "lg0":
                                dst, bv, bi, k = P0[:], b4, bias0, H
                            else:
                                i = int(name[-1])
                                dst, bv, bi, k = P1[:, 2 * i:2 * i + 2, :], b[:].rearrange("p (h d) -> p h d", h=2), bias1, 2
                            w = P if name == "lg0" else S
                            v_.scalar_tensor_tensor(out=dst, in0=bv, scalar=SCALE,
                                                    in1=bi[:].unsqueeze(1).to_broadcast([P, k, w]), op0=ALU.mult,
                                                    op1=ALU.add).then_inc(fa, 1)
                            if name == "lg1_1":
                                dve.wait_ge(*result(upto, "lg1_0"))
                                dve.wait_ge(*result(upto, "lg1_1"))
                                v_.tensor_reduce(nm1[:], P1[:], AX.X, ALU.max, negate=True).then_inc(biased1, 1)
                            if name == "lg0":
                                dve.wait_ge(*result(upto, "lg0"))
                                v_.tensor_reduce(nm0[:], P0[:], AX.X, ALU.max, negate=True).then_inc(biased0, 1)
                        if name in ("pv1", "pv0", "mv0", "mv1"):
                            t = int(name[2])
                            dve.wait_ge(stepped, upto(stepped, n + 1))
                            link(v_.reciprocal(ri[:], (su0, su1)[t][:]))
                            v_.tensor_tensor(obuf[:, B_DSA if name[0] == "p" else B_MEM, t, :]
                                             .rearrange("p (h d) -> p h d", h=H), b4,
                                             ri[:].unsqueeze(2).to_broadcast([P, H, HD]), ALU.mult).then_inc(fa, 1)
                            dve.wait_ge(*result(upto, name))
                        if name in ("at0", "at1"):
                            dve.wait_ge(stepped, upto(stepped, n + 1))
                            if name == "at1":
                                dve.wait_ge(stepped, upto(stepped, NUM["go0"] + 1))
                            v_.copy_predicated(attn[:], tri[:].bitcast(I32).unsqueeze(1).to_broadcast([P, H, P]), b4)\
                                .then_inc(fa, 1)
                        if name == "dS0":
                            dve.wait_ge(stepped, upto(stepped, n + 1))
                            dve.wait_ge(*result(upto, "dec"))
                            bv = b[:].rearrange("p (c h e) -> p c h e", c=2, h=2)
                            link(v_.tensor_copy(stt_[:, 0], bv[:, 0]))
                            for hp in range(2):
                                ins = v_.scalar_tensor_tensor(out=stt_[:, 1, hp, :], in0=stt_[:, 0, hp, :],
                                                              scalar=dec[:, hp, 1:2], in1=bv[:, 1, hp, :], op0=ALU.mult,
                                                              op1=ALU.add)
                            ins.then_inc(fa, 1)
                            dve.wait_ge(*result(upto, "dS0"))
                        if name == "dS1":
                            dve.wait_ge(stepped, upto(stepped, n + 1))
                            for hp in range(2):
                                ins = v_.scalar_tensor_tensor(out=stt_[:, 2, hp, :], in0=stt_[:, 1, hp, :],
                                                              scalar=dec[:, hp, 2:3], in1=b[:, hp * P:(hp + 1) * P],
                                                              op0=ALU.mult, op1=ALU.add)
                            ins.then_inc(fa, 1)
                        if name in ("go0", "go1"):
                            dve.wait_ge(stepped, upto(stepped, n + 1))
                            v_.tensor_copy(obuf[:, B_GLA, int(name[2]), :], b[:]).then_inc(fa, 1)
                        if name in ("cumD", "cumT", "cumL"):
                            dve.wait_ge(*result(upto, name))
                            if name == "cumD":
                                dve.wait_ge(taken, upto(taken, G_GQK + 1))
                            gq, gk = E2[:, :, 0:S], E2[:, :, S:2 * S]
                            if name == "cumD":
                                v_.scalar_tensor_tensor(out=t1[:], in0=gq, scalar=GD ** -0.5, in1=t1[:], op0=ALU.mult,
                                                        op1=ALU.mult)
                                v_.tensor_tensor(t2[:], gk, t2[:], ALU.mult).then_inc(gmul, 1)
                            elif name == "cumT":
                                v_.scalar_tensor_tensor(out=t3[:], in0=gq, scalar=GD ** -0.5, in1=t3[:], op0=ALU.mult,
                                                        op1=ALU.mult).then_inc(gmul, 1)
                            else:
                                v_.tensor_tensor(kd[:], gk, kd[:], ALU.mult).then_inc(gmul, 1)
                        if name[:2] == "ml":
                            t, i = int(name[2]), int(name[4])
                            dve.wait_ge(stepped, upto(stepped, n + 1))
                            nm = (nm0, nm1)[t][:, 2 * i:2 * i + 2]
                            link(v_.tensor_reduce(nm, b[:].rearrange("p (h d) -> p h d", h=2), AX.X, ALU.max, negate=True))
                            v_.tensor_scalar(nm, nm, SCALE, None, ALU.mult).then_inc(mmax, 1)
                        if name[:3] == "glu":
                            t = int(name[3])
                            dve.wait_ge(*result(upto, name))
                            dve.wait_ge(*result(upto, f"yt{t}"))
                            link(v_.tensor_scalar(gt[:, t, :], gt[:, t, :], 0.5, 0.5, ALU.mult, ALU.add))
                            ins = v_.tensor_tensor(obuf[:, B_S5, t, :], gt[:, t, :], obuf[:, B_S5, t, :], ALU.mult)
                            if t == 1:
                                ins.then_inc(obr, 1)
                    if s in BU:
                        j = BU[s]
                        b, jj = divmod(j, TB)
                        dve.wait_ge(wroteB, upto(wroteB, BBU + j + 1))
                        if jj == 0:
                            dve.wait_ge(phased, upto(phased, b + 1))
                        bb = bankB[:].rearrange("p (i s) -> p i s", i=2)
                        for i in (1, 0):
                            ins = v_.tensor_tensor(rot[:, i], bb, tab[:, b % 2, i, jj, :].unsqueeze(1)
                                                   .to_broadcast([P, 2, S]), ALU.mult)
                        ins.then_inc(freeB, 1)
                        dve.wait_ge(freeB, upto(freeB, BBU + j + 1))
                        if j >= 2:
                            dve.wait_ge(unrot, upto(unrot, j - 1))
                        z = vz[:, j % 2]
                        v_.tensor_tensor(z[:, 0], rot[:, 1, 0], rot[:, 0, 1], ALU.add)
                        link(v_.tensor_tensor(z[:, 1], rot[:, 1, 1], rot[:, 0, 0], ALU.subtract))
                        for i in range(2):
                            ins = v_.tensor_tensor_scan(z[:, i], s5[:, 5, j:j + 1].to_broadcast([P, S]), z[:, i], 0.0,
                                                        ALU.mult, ALU.add)
                        ins.then_inc(scanned, 1)
                    for ct in range(4):
                        base = S5_SLOT[4 * ct + 3] + S5_LAG
                        y = ych[:, ct, :]
                        if s == base + 1:
                            dve.wait_ge(yprod, upto(yprod, 4 * ct + 4))
                            if l == 0 and ct == 0:
                                dve.wait_ge(k_out[1], 16)
                            link(v_.scalar_tensor_tensor(out=y, in0=uT[:, ct, :], scalar=col("d", ct),
                                                         in1=bankY[:, ct % 2, :], op0=ALU.mult, op1=ALU.add))
                            link(v_.tensor_tensor(ytmp[:], y, y, ALU.mult))
                            link(v_.tensor_scalar(ytmp[:], ytmp[:], 0.044715, 1.0, ALU.mult, ALU.add))
                            v_.tensor_tensor(ytmp[:], ytmp[:], y, ALU.mult).then_inc(ypoly, 1)
                            dve.wait_ge(ypoly, upto(ypoly, ct + 1))
                            link(v_.tensor_scalar(y, y, 0.5, None, ALU.mult))
                        if s == base + 3:
                            dve.wait_ge(ytanh, upto(ytanh, ct + 1))
                            v_.scalar_tensor_tensor(out=y, in0=ytmp[:], scalar=1.0, in1=y, op0=ALU.add,
                                                    op1=ALU.mult).then_inc(gelud, 1)
                            dve.wait_ge(gelud, upto(gelud, ct + 1))
                    if c == 0 and 9 <= g <= 12:
                        z = g - 9
                        dve.wait_ge(ztanh, upto(ztanh, z + 1))
                        for t in range(NT):
                            ins = v_.scalar_tensor_tensor(out=Ez[:, t, :], in0=Ez[:, t, :], scalar=1.0,
                                                          in1=acc[(g - 1) % 2][t][:], op0=ALU.add, op1=ALU.mult)
                        ins.then_inc(gated, 1)
                        dve.wait_ge(gated, upto(gated, z + 1))
                    if s in (73, 81, 95, 96):
                        z = (73, 81, 95, 96).index(s)
                        dve.wait_ge(normr, upto(normr, {B_DSA: SQ_DSA, B_GLA: SQ_GLA, B_S5: SQ_S5, B_MEM: SQ_MEM}[z] + 1))
                        for t in range(NT):
                            ins = v_.scalar_tensor_tensor(out=obuf[:, z, t, :], in0=Ez[:, t, :], scalar=rsh[:, t:t + 1],
                                                          in1=obuf[:, z, t, :], op0=ALU.mult, op1=ALU.mult)
                        ins.then_inc(zmul, 1)
                    if s in (104, 112, 120):
                        x_add(l, (s - 104) // 8)
            x_add(L - 1, 3)


def kernel(**inputs):
    import numpy as _np
    import concourse.bacc as _bacc
    from concourse import mybir as _mybir
    from concourse.bass_utils import run_bass_kernel_spmd as _run

    a = {k: _np.asarray(v) for k, v in inputs.items()}

    def chunks(w, k0=0):
        w = _np.concatenate([w, _np.zeros((D, W - w.shape[1]), w.dtype)], 1)
        return w.reshape(NC, CK, P, W).transpose(0, 2, 1, 3).reshape(NC, P, CK * W)

    parts = []
    for l in range(L):
        parts += [chunks(a["w_mem_kv"][l][:, :W]), chunks(a["w_mem_kv"][l][:, W:])]
    rows = _np.r_[1024:1536, 0:512, 512:1024, 1536:2048]
    for l in range(L):
        w = a["w_in"][l]

        def cut(name, n):
            return w[:, IN[name]:IN[name] + n]
        for p in (cut("iq", W), w[:, IN["iq"] + W:IN["iq"] + 2 * W],
                  _np.concatenate([cut("dk", 256), cut("ik", 64), cut("iw", 16), cut("glr", 16)], 1),
                  cut("su", W), cut("dq", W), cut("gq", W), cut("gv", W), cut("mq", W),
                  cut("dz", W), cut("gz", W), cut("sz", W), cut("mz", W)):
            parts.append(chunks(p))
        wo = a["w_out"][l][rows]
        parts += [chunks(wo[:, i * W:(i + 1) * W]) for i in range(4)]
    stream = _np.concatenate(parts, 0)

    def rows_of(v):
        return v.reshape(-1, P).T

    def states(v):
        return v.reshape(ST, P).T

    def wide(v):
        return _np.broadcast_to(v, (P, v.shape[0]))
    par = _np.stack([_np.concatenate([
        rows_of(a["ln_gain"][l]), rows_of(a["out_norm"][l][rows]), states(a["s5_a_re"][l]), states(a["s5_a_im"][l]),
        states(_np.broadcast_to(a["s5_log_step"][l][:, None], (32, 64))), rows_of(a["s5_d"][l]),
        a["mem_q_norm"][l][:, None], wide(a["dsa_q_norm"][l]), wide(a["dsa_k_norm"][l]), wide(a["gla_b_up"][l])], 1)
        for l in range(L)])
    mgain = _np.stack([_np.concatenate([rows_of(a["mem_norm"][l]), a["mem_k_norm"][l][:, None]], 1)
                       for l in range(L)], 1)
    bmat = _np.zeros((L, P, 4, 2, P), _np.float32)
    cmat = _np.zeros((L, P, ST, 2, 32), _np.float32)
    for i, (bn, cn) in enumerate((("s5_b_re", "s5_c_re"), ("s5_b_im", "s5_c_im"))):
        for gg in range(2):
            b = a[bn].reshape(L, 4, 4, 2, 64, 16)[:, :, :, gg]
            for jj in range(4):
                r = 32 * jj + 16 * gg
                bmat[:, r:r + 16, :, i, 64 * gg:64 * gg + 64] = b[:, :, jj].transpose(0, 3, 1, 2)
            c = a[cn].reshape(L, ST, 2, 16, 64)[:, :, gg]
            cmat[:, 64 * gg:64 * gg + 64, :, i, 16 * gg:16 * gg + 16] = c.transpose(0, 3, 1, 2)
    wglu = a["s5_w_glu"].reshape(L, 4, P, W).transpose(0, 2, 1, 3).reshape(L, P, 4 * W)
    invf = _np.concatenate([_np.float32(500000.0) ** (-_np.arange(n, dtype=_np.float32) * _np.float32(2.0)
                                                      / _np.float32(2 * n)) for n in (8, 16)]).astype(_np.float32)
    pos = a["positions"].reshape(NT, P).T
    sent = dict(stream=stream, mem=a["mem"][0], x=a["x"][0], pos=pos, invf=invf, mgain=mgain, par=par, bmat=bmat,
                cmat=cmat, wup=a["gla_w_up"], wglu=wglu)
    sent = {k: _np.ascontiguousarray(v) for k, v in sent.items()}

    nc = _bacc.Bacc("TRN2", target_bir_lowering=False, num_devices=1)
    args = {k: nc.dram_tensor(f"in_{k}", v.shape, _mybir.dt.from_np(v.dtype), kind="ExternalInput").ap()
            for k, v in sent.items()}
    out = nc.dram_tensor("out_0", (S, D), _mybir.dt.float32, kind="ExternalOutput").ap()
    build(nc, out=out, **args)
    r = _run(nc, [{f"in_{k}": v for k, v in sent.items()}], core_ids=[0])
    return r.results[0]["out_0"].reshape(a["x"].shape)
```

```python
import math
from contextlib import ExitStack

import numpy as np
import concourse.bass as bass
from concourse import mybir

ALU = mybir.AluOpType
ACT = mybir.ActivationFunctionType
AX = mybir.AxisListType
F32 = mybir.dt.float32
F32R = mybir.dt.float32r
I32 = mybir.dt.int32

P = 128
L = 2
D = 2048
S = 256
NT = S // P
KT = D // P
W = 512
CK = 2
NC = KT // CK
GROUPS = 16
SLOTS = GROUPS * NC
PRO_GROUPS = 2 * L
PRO = PRO_GROUPS * NC
RING = 4
AHEAD = 3
EPS = 1e-6
H = 4
HD = 128
GD = 64
IH, ID = 16, 64
TOPK = 64
ST = 16
TB = 4
MAGIC = 1.5 * 2.0 ** 23
TWO_PI = 2 * math.pi
TURN = 6.283185
GELU_CUBE = 0.044715
NEG = -3.0e38
TAKEN = -3.4e38
BIG = 1.0e30
IN = dict(gq=0, gk=256, gv=512, glr=1024, gz=1040, su=1552, sz=2064, dq=2576, dk=3088, dv=3216,
          iq=3344, ik=4368, iw=4432, dz=4448, mq=4960, mz=5472, end=5984)
MISC = dict(dk=0, dv=128, ik=256, iw=320, glr=336, end=352)
G_SU, G_IQ0, G_IQ1, G_MISC, G_DQ, G_GQK, G_GV, G_MQ, G_Z, G_OUT = 0, 1, 2, 3, 4, 5, 6, 7, 8, 12
B_DSA, B_GLA, B_S5, B_MEM = 0, 1, 2, 3
PC = dict(ln=0, on=16, are=32, aim=48, lst=64, d=80, mqg=84, qg=85, kg=213, bup=341, end=597)
MG = dict(mn=0, mk=16, end=17)

STEPS = [("uT0", 10), ("uT1", 11), ("iqT0", 20), ("iqT1", 21), ("iqT2", 28), ("iqT3", 29), ("ikT", 37), ("glrT", 38),
         ("gate", 39)]
STEPS += [(f"rel1_{i}", 40 + i) for i in range(8)] + [(f"rel0_{i}", 48 + i) for i in range(4)]
STEPS += [("qT0", 52), ("qT1", 53), ("cumD", 54), ("cumT", 55), ("cumL", 56), ("dec", 57), ("qbT", 58),
          ("lg1_0", 59), ("lg1_1", 60), ("lg0", 61), ("qeT", 62), ("keT", 63), ("pT1_0", 64), ("pT1_1", 65), ("pv1", 66),
          ("pT0", 67), ("pv0", 68), ("dS0", 69), ("dS1", 70), ("at0", 71), ("mqT0", 72), ("go0", 73), ("at1", 74),
          ("mqT1", 75), ("go1", 76), ("ml0_0", 77), ("ml0_1", 78), ("yt0", 79), ("yt1", 80), ("glu0", 81),
          ("mp0_0", 82), ("mp0_1", 83), ("glu1", 84), ("mv0", 85), ("ml1_0", 86), ("ml1_1", 87), ("mp1_0", 89),
          ("mp1_1", 90), ("mv1", 91)]
AT = {slot: name for name, slot in STEPS}
NUM = {name: n for n, (name, _) in enumerate(STEPS)}
NA = len(STEPS)
assert len(AT) == NA
PRO_A = 2 * L
S5_SLOT = [14 + 15 * j // 4 for j in range(ST)]
S5_LAG = 5
FRAC_SLOT = (6, 23, 34, 43)
SIN_SLOT = (9, 26, 36, 46)
BU = {s: j for j, s in enumerate(S5_SLOT)}
YS = {s + S5_LAG: j for j, s in enumerate(S5_SLOT)}
TURN_O = {90: 0, 91: 1, 92: 2, 93: 3, 94: 4, 95: 5, 99: 6, 100: 7}
TURN_N = {122 + c: c for c in range(6)}
TURN_X = {2: 6, 3: 7}
POOL_LO = (54, 58, 62)
BX, BBU, BO, BN = 0, 2, 2 + ST, 2 + ST + 8
NB = BN + 6
SLOT = dict(STEPS)
XB = 3
SQUARE_P = (24, 25, 28)
MEM_SQUARE = range(4, 12)
KV_COPY, KV_TURN, KV_READ = {13: 0, 26: 1}, {17: 0, 30: 1}, {18: 0, 31: 1}
TURN_P = {20: 0, 21: 1, 22: 2, 23: 3, 26: 4, 27: 5}
SQ_DQ, SQ_MQ, SQ_DSA, SQ_GLA, SQ_S5, SQ_MEM = range(6)
NORM_SLOT = (41, 66, 69, 77, 86, 92)
TOP1 = range(48, 48 + TOPK // 8)
TOP0 = range(52, 52 + TOPK // 8)
ZMUL_SLOT = (73, 81, 90, 97)
SCALE = HD ** -0.5


def build(nc, stream, mem, x, pos, invf, mgain, par, bmat, cmat, wup, wglu, out):
    ctx = ExitStack()
    with ctx:
        top = [16640]
        placed = {}

        def at(name, shape, dt, offset=None):
            size = int(np.prod(shape[1:])) * 4
            if offset is None:
                offset = top[0]
                top[0] += (size + 31) // 32 * 32
            placed[name] = offset
            return nc.alloc_sbuf_tensor_at(name, shape, dt, offset=offset)

        raw = at("raw", [P, RING, CK * W], F32)
        whi = at("whi", [P, RING, CK * W], F32R)
        wlo = at("wlo", [P, RING, CK * W], F32R)
        hhi = at("hhi", [P, KT, S], F32R)
        hlo = at("hlo", [P, KT, S], F32R)
        tab = at("tab", [P, 2, 2, TB, S], F32)
        obuf = at("obuf", [P, 4, NT, W], F32)
        wg = at("wg", [P, 4, W], F32, placed["tab"])
        mhi = at("mhi", [P, KT, S], F32R, placed["tab"])
        mlo = at("mlo", [P, KT, S], F32R, placed["obuf"])
        iq = at("iq", [P, NT, IH * ID], F32, placed["obuf"])
        iqT = at("iqT", [P, IH // 2, S], F32, placed["obuf"] + 8192)
        P0 = at("P0", [P, H, P], F32, placed["obuf"] + 8192)
        P1 = at("P1", [P, H, S], F32, placed["obuf"] + 12288)
        xr = at("xr", [P, XB, NT, W], F32)
        uT = at("uT", [P, 4, S], F32)
        ych = at("ych", [P, 4, S], F32)
        kvT = at("kvT", [P, H, S], F32, placed["ych"])
        rot = at("rot", [P, 2, 2, S], F32)
        vz = at("vz", [P, 2, 2, S], F32)
        qq = at("qq", [P, 2, 2, S], F32)
        xs = at("xs", [P, 2, 2, S], F32)
        ytmp = at("ytmp", [P, S], F32)
        gt = at("gt", [P, NT, W], F32, placed["rot"])
        bm = at("bm", [P, 4, 2, P], F32)
        cp = at("cp", [P, ST, 2, 32], F32)
        pa = at("pa", [P, PC["end"]], F32)
        wu = at("wu", [16, S], F32)
        E1 = at("E1", [P, NT, W], F32)
        E2 = at("E2", [P, NT, W], F32)
        Pm = at("Pm", [P, H, S], F32, placed["E2"])
        E3 = at("E3", [P, NT, W], F32)
        la = at("la", [P, NT, S], F32)
        kkT = at("kkT", [P, 2, S], F32)
        Ez = at("Ez", [P, NT, W], F32, placed["la"])
        memr = at("memr", [P, NT, D], F32, placed["E1"])
        assert placed["la"] == placed["E1"] + 12288
        R1 = at("R1", [P, 2, W], F32)
        rel = R1
        pT = at("pT", [P, H, NT, P], F32, placed["R1"])
        R2 = at("R2", [P, H, S], F32)
        qT = R2
        qeT = at("qeT", [P, 2, S], F32, placed["R2"])
        keT = at("keT", [P, 2, S], F32, placed["R2"] + 2048)
        qbT = at("qbT", [P, 2, S], F32)
        t1 = at("t1", [P, NT, S], F32, placed["xr"])
        t2 = at("t2", [P, NT, S], F32, placed["xr"] + 2048)
        t3 = at("t3", [P, NT, S], F32, placed["xr"] + 4096)
        kd = at("kd", [P, NT, S], F32, placed["xr"] + 6144)
        mqT = at("mqT", [P, H, S], F32, placed["t1"])
        mkT = at("mkT", [P, H, S], F32, placed["t3"])
        mv = at("mv", [P, NT, W], F32, placed["E1"])
        sc = at("sc", [P, S], F32)
        sc0 = at("sc0", [P, P], F32)
        bias1 = at("bias1", [P, S], F32)
        bias0 = at("bias0", [P, P], F32)
        stt_ = at("Sst", [P, 3, 2, P], F32, placed["xr"] + 8192)
        attn = at("attn", [P, H, P], F32)
        misc = at("misc", [P, NT, MISC["end"]], F32)
        ikd = at("ikd", [P, NT, P], F32)
        rt = at("rt", [P, 4, NT * 8 * 8], F32)
        ident = at("ident", [P, P], F32)
        c01 = at("c01", [P, S], F32)
        negm = at("negm", [P, S], F32)
        tri = at("tri", [P, P], F32)
        triM = at("triM", [P, P], F32)
        triL = at("triL", [P, P], F32)
        cind = at("cind", [P, 2], F32)
        tvec = at("tvec", [P, S], F32)
        tint = at("tint", [P, S], I32, placed["vz"])
        mg = at("mg", [P, L, MG["end"]], F32)
        frq = at("frq", [P, 24], F32)
        posi = at("posi", [P, NT], I32)
        posf = at("posf", [P, NT], F32)
        ang = at("ang", [P, 4, NT, 24], F32, placed["qq"])
        snc = at("snc", [P, 2, NT, 24], F32)
        half = at("half", [P, 8], F32)
        quarter = at("quarter", [P, 1], F32)
        warm = at("warm", [P, 1], F32)
        ssx = at("ssx", [P, NT, 4], F32)
        rs = at("rs", [P, NT], F32)
        rsh = at("rsh", [P, NT], F32)
        ssm = at("ssm", [P, NT, 4], F32)
        rm = at("rm", [P, NT], F32)
        sq8 = at("sq8", [P, 8], F32)
        r8 = at("r8", [P, 8], F32)
        sqk = at("sqk", [P, NT], F32)
        rk = at("rk", [P, NT], F32)
        mx8 = at("mx8", [P, 8], F32)
        nm1 = at("nm1", [P, H], F32)
        nm0 = at("nm0", [P, H], F32)
        su1 = at("su1", [P, H], F32)
        su0 = at("su0", [P, H], F32)
        ri = at("ri", [P, H], F32)
        s5 = at("s5", [P, 16, ST], F32)
        dec = at("dec", [P, 2, 4], F32)
        assert top[0] <= 229368, top[0]

        acc = [[ctx.enter_context(nc.psum_tensor(f"acc{g}{t}", [P, W], F32)) for t in range(NT)] for g in range(2)]
        bankA = [ctx.enter_context(nc.psum_tensor(f"bankA{i}", [P, W], F32)) for i in range(2)]
        bankB = ctx.enter_context(nc.psum_tensor("bankB", [P, W], F32))
        bankY = ctx.enter_context(nc.psum_tensor("bankY", [P, 2, S], F32))

        kvs = nc.dram_tensor("kvs", [L, 2, P, 1024], F32, kind="Internal").ap()
        xsc = nc.dram_tensor("xsc", [P, NT, D], F32, kind="Internal").ap()

        counts = {}

        def sem(name, pro, per):
            s = ctx.enter_context(nc.semaphore(name))
            counts[s.name] = (pro, per)
            return s

        landed = [sem(f"landed{i}", 16 * PRO // RING, 16 * SLOTS // RING) for i in range(RING)]
        hi_done = sem("hi_done", PRO, SLOTS)
        lo_done = sem("lo_done", PRO, SLOTS - len(POOL_LO))
        lo_pool = sem("lo_pool", 0, len(POOL_LO))
        used = sem("used", PRO, SLOTS)
        taken = sem("taken", PRO_GROUPS, 8)
        gated = sem("gated", 0, 4)
        added = sem("added", 0, 4)
        stepped = sem("stepped", PRO_A, NA)
        freeA = [sem(f"freeA{i}", PRO_A // 2, NA // 2) for i in range(2)]
        wroteB = sem("wroteB", NC + 6, NB)
        turned_hi = sem("turned_hi", NC + 6, 16)
        freeB = sem("freeB", NC + 6, NB)
        par_in = sem("par_in", 0, 64)
        glu_in = sem("glu_in", 0, 16)
        mk_in = sem("mk_in", 0, 16)
        mv_in = sem("mv_in", 0, 16)
        tile_done = sem("tile_done", 0, 0)
        last_added = sem("last_added", 0, 0)
        x_in = sem("x_in", 64, 64)
        x_out = sem("x_out", 0, 64)
        k_out = [sem(f"k_out{i}", 16, 0) for i in range(L)]
        v_out = [sem(f"v_out{i}", 16, 0) for i in range(L)]
        mem_in = [sem(f"mem_in{i}", 16, 0) for i in range(4)]
        mg_in = sem("mg_in", 16, 0)
        const_in = sem("const_in", 32, 0)
        ident_ready = sem("ident_ready", 1, 0)
        consts = sem("consts", 1, 0)
        ang_ready = sem("ang_ready", 1, 0)
        rope_ready = sem("rope_ready", 1, 0)
        sq_mem = sem("sq_mem", 1, 0)
        rm_sum = sem("rm_sum", 1, 0)
        rm_done = sem("rm_done", 1, 0)
        sq_kv = sem("sq_kv", L, 0)
        kv_sum = sem("kv_sum", L, 0)
        kv_norm = sem("kv_norm", L, 0)
        sq_x = sem("sq_x", 3, 4)
        rs_sum = sem("rs_sum", 0, 1)
        rs_done = sem("rs_done", 0, 1)
        roped_iq = sem("roped_iq", 0, 2)
        k_sum = sem("k_sum", 0, 1)
        roped_k = sem("roped_k", 0, 1)
        roped_q = sem("roped_q", 0, 1)
        weighed = sem("weighed", 0, 12)
        biased1 = sem("biased1", 0, 1)
        biased0 = sem("biased0", 0, 1)
        exp1 = sem("exp1", 0, 1)
        exp0 = sem("exp0", 0, 1)
        mmax = sem("mmax", 0, 4)
        lsoft = sem("lsoft", 0, 1)
        lsum = sem("lsum", 0, 1)
        gmul = sem("gmul", 0, 3)
        squared = sem("squared", 0, 6)
        sq_read = sem("sq_read", 0, 6)
        normr = sem("normr", 0, 6)
        obr = sem("obr", 0, 1)
        s5_exp = sem("s5_exp", 0, 1)
        s5_phase = sem("s5_phase", 0, 1)
        s5_sin = sem("s5_sin", 0, 1)
        s5_c = sem("s5_c", 0, 1)
        frac = sem("frac", 0, 4)
        phased = sem("phased", 0, 4)
        scanned = sem("scanned", 0, ST)
        unrot = sem("unrot", 0, ST)
        yprod = sem("yprod", 0, ST)
        ypoly = sem("ypoly", 0, 4)
        ytanh = sem("ytanh", 0, 4)
        gelud = sem("gelud", 0, 4)
        ztanh = sem("ztanh", 0, 4)
        zmul = sem("zmul", 0, 4)
        dve_own = sem("dve_own", 0, 0)
        act_own = sem("act_own", 0, 0)
        pe_own = sem("pe_own", 0, 0)
        pool_own = sem("pool_own", 0, 0)

        def counter(l):
            def upto(s, n):
                before, each = counts[s.name]
                return n if l is None else before + l * each + n
            return upto

        def linker(eng, s):
            count = [0]

            def link(ins):
                count[0] += 1
                ins.then_inc(s, 1)
                eng.wait_ge(s, count[0])
            return link

        def col(name, i=0):
            return pa[:, PC[name] + i:PC[name] + i + 1]

        def result(upto, name):
            s = freeA[NUM[name] % 2]
            return s, upto(s, NUM[name] // 2 + 1)

        def low_part(l, n):
            if l is not None and n < 0:
                l, n = (l - 1, n + SLOTS) if l else (None, n + PRO)
            if l is not None and n in POOL_LO:
                return lo_pool, counter(l)(lo_pool, POOL_LO.index(n) + 1)
            return lo_done, counter(l)(lo_done, n + 1 - (sum(k < n for k in POOL_LO) if l is not None else 0))

        assert NA % 2 == 0

        def memory_bank(c):
            return bankY[:].rearrange("p a s -> p (a s)") if c % 2 else bankB[:]

        def bank_of(name):
            return bankA[NUM[name] % 2]

        block = ctx.enter_context(nc.Block())

        @block.sync
        def _(sp):
            xv = x.rearrange("(t p) d -> p t d", p=P)
            ov = out.rearrange("(t p) d -> p t d", p=P)

            def flat(t):
                return t[:].rearrange("p a b -> p (a b)")

            def chunk(n, l):
                upto = counter(l)
                if l is not None or n >= RING:
                    sp.wait_ge(hi_done, upto(hi_done, n - RING + 1))
                    sp.wait_ge(*low_part(l, n - RING))
                total = n if l is None else PRO + SLOTS * l + n
                sp.dma_start(raw[:, n % RING, :], stream[total]).then_inc(landed[n % RING], 16)

            def params(l):
                if l >= 1:
                    sp.wait_ge(freeB, counter(l - 1)(freeB, BO + 8))
                sp.dma_start(pa[:], par[l]).then_inc(par_in, 16)
                sp.dma_start(bm[:], bmat[l]).then_inc(par_in, 16)
                sp.dma_start(cp[:], cmat[l]).then_inc(par_in, 16)
                sp.dma_start(wu[:], wup[l]).then_inc(par_in, 16)

            def x_load(l, g):
                src = xv if not l else xsc
                sp.dma_start(xr[:, g % XB], src[:, :, g * W:(g + 1) * W]).then_inc(x_in, 16)

            def x_store(l, g):
                dst = ov if l == L - 1 else xsc
                if (l, g) == (L - 1, 3):
                    for t in range(NT):
                        sp.wait_ge(last_added, t + 1)
                        sp.dma_start(dst[:, t, g * W:(g + 1) * W], xr[:, g % XB, t]).then_inc(x_out, 16)
                    return
                sp.wait_ge(added, counter(l)(added, g + 1))
                sp.dma_start(dst[:, :, g * W:(g + 1) * W], xr[:, g % XB]).then_inc(x_out, 16)

            def x_load3(l):
                upto = counter(l)
                sp.wait_ge(x_out, upto(x_out, 48))
                if l + 1 < L:
                    sp.wait_ge(wroteB, upto(wroteB, BN + 2))
                    sp.wait_ge(sq_x, upto(sq_x, 2))
                x_load(l, 3)

            upto = counter(None)
            memv = mem.rearrange("(t p) d -> p t d", p=P)
            for n in range(RING):
                sp.dma_start(memr[:, :, n * W:(n + 1) * W], memv[:, :, n * W:(n + 1) * W]).then_inc(mem_in[n], 16)
                if n == 0:
                    sp.dma_start(mg[:], mgain).then_inc(mg_in, 16)
                chunk(n, None)
            sp.dma_start(frq[:], invf.partition_broadcast(P)).then_inc(const_in, 16)
            sp.dma_start(posi[:], pos).then_inc(const_in, 16)
            for n in range(RING, PRO):
                chunk(n, None)
                if n == 9:
                    params(0)
                if n in (11, 13, 15):
                    x_load(None, (n - 11) // 2)
                if n == 27:
                    sp.wait_ge(freeA[1], upto(freeA[1], 1))
                    sp.dma_start(kvs[0, 0], flat(kvT)).then_inc(k_out[0], 16)
                if n == 25:
                    sp.wait_ge(taken, upto(taken, 2))
                    sp.dma_start(kvs[0, 1], flat(R1)).then_inc(v_out[0], 16)
                if n == 31:
                    sp.wait_ge(wroteB, upto(wroteB, NC + 2))
                    sp.wait_ge(sq_x, upto(sq_x, 1))
                    x_load(None, 3)
            for l in range(L):
                upto = counter(l)
                for n in range(SLOTS):
                    chunk(n, l)
                    if n == 4 and l > 0:
                        x_load3(l - 1)
                    if n == 6 and l == 0:
                        sp.wait_ge(freeA[1], counter(None)(freeA[1], 2))
                        sp.dma_start(kvs[1, 0], flat(kvT)).then_inc(k_out[1], 16)
                    if n == 10 and l == 0:
                        sp.wait_ge(taken, counter(None)(taken, 4))
                        sp.dma_start(kvs[1, 1], flat(R1)).then_inc(v_out[1], 16)
                    if n == 10 and l > 0:
                        x_store(l - 1, 3)
                    if n == 102:
                        sp.wait_ge(stepped, upto(stepped, NUM["ml1_1"] + 1))
                        if l > 0:
                            sp.wait_ge(x_out, upto(x_out, 0))
                        for g in range(3):
                            x_load(l, g)
                    if n == 78:
                        sp.wait_ge(k_out[l], 16)
                        sp.wait_ge(stepped, upto(stepped, NUM["dS1"] + 1))
                        sp.dma_start(flat(mkT), kvs[l, 0]).then_inc(mk_in, 16)
                    if n == 84:
                        sp.wait_ge(stepped, upto(stepped, NUM["go1"] + 1))
                        sp.wait_ge(v_out[l], 16)
                        sp.dma_start(flat(mv), kvs[l, 1]).then_inc(mv_in, 16)
                    if n == 79:
                        sp.wait_ge(unrot, upto(unrot, ST))
                        sp.dma_start(flat(wg), wglu[l]).then_inc(glu_in, 16)
                    if n == 113 and l + 1 < L:
                        params(l + 1)
                    if n in (112, 120):
                        x_store(l, (n - 112) // 8)
                    if n == 2 and l > 0:
                        x_store(l - 1, 2)
            x_store(L - 1, 2)
            x_load3(L - 1)
            x_store(L - 1, 3)
            sp.wait_ge(x_out, 64 * L + 16 * (NT - 1))

        @block.gpsimd
        def _(pool):
            link = linker(pool, pool_own)
            upto = counter(None)
            g = nc.gpsimd
            link(g.memset(ident[:], 0.0))
            g.affine_select(out=ident[:], in_=ident[:], compare_op=ALU.not_equal, fill=1.0, base=0,
                            pattern=[[-1, P]], channel_multiplier=1).then_inc(ident_ready, 1)
            for z in (tri, triM, triL, cind, attn):
                g.memset(z[:], 0.0)
            g.memset(c01[:], 1.0)
            g.memset(half[:], -0.5)
            g.memset(quarter[:], 0.5 * math.pi)
            link(g.iota(tint[:], [[1, S]], base=0, channel_multiplier=0))
            link(g.tensor_copy(tvec[:], tint[:]))
            link(g.affine_select(out=c01[:], in_=c01[:], compare_op=ALU.is_ge, fill=0.0, base=P,
                                 pattern=[[-1, S]], channel_multiplier=1))
            link(g.tensor_scalar(negm[:], c01[:], 1.0, -NEG, ALU.subtract, ALU.mult))
            link(g.affine_select(out=tri[:], in_=tri[:], compare_op=ALU.is_gt, fill=1.0, base=0,
                                 pattern=[[-1, P]], channel_multiplier=1))
            link(g.memset(tri[0:GD, GD:P], 0.0))
            for c in range(2):
                a = GD * c
                g.memset(triM[a:a + GD // 2 + 1, a:a + GD], 1.0)
                g.memset(triL[a:a + GD, a:a + GD], 1.0)
                link(g.memset(cind[a:a + GD, c:c + 1], 1.0))
            link(g.tensor_tensor(triM[:], tri[:], triM[:], ALU.subtract))
            g.tensor_tensor(triL[:], triL[:], tri[:], ALU.subtract).then_inc(consts, 1)

            def rstd(out_, in_, n, width):
                link(g.tensor_scalar(out_, in_, 1.0 / n, EPS, ALU.mult, ALU.add))
                return g.tensor_tensor(out_, out_, half[:, 0:width], ALU.pow)

            pool.wait_ge(const_in, upto(const_in, 32))
            link(g.tensor_copy(posf[:], posi[:]))
            for t in range(NT):
                link(g.tensor_scalar(ang[:, 3, t, :], frq[:], posf[:, t:t + 1], None, ALU.mult))
            c1 = 6.28125
            c2 = float(np.float32(np.round((TWO_PI - c1) * 2 ** 19) / 2 ** 19))
            c3 = TWO_PI - c1 - c2
            for i in range(2):
                link(g.tensor_scalar(ang[:, 2], ang[:, 3], 1.0 / TWO_PI, 0.25 * i, ALU.mult, ALU.add))
                link(g.tensor_scalar(ang[:, 2], ang[:, 2], MAGIC, None, ALU.add))
                link(g.tensor_scalar(ang[:, 2], ang[:, 2], MAGIC, None, ALU.subtract))
                first = True
                for c in (c1, c2, c3):
                    link(g.tensor_scalar(snc[:, 0], ang[:, 2], -c, None, ALU.mult))
                    link(g.tensor_tensor(ang[:, i], ang[:, 3] if first else ang[:, i], snc[:, 0], ALU.add))
                    first = False
                link(g.tensor_scalar(ang[:, i], ang[:, i], 0.5 * math.pi * i, 3.1415925, ALU.add, ALU.min))
                link(g.tensor_scalar(ang[:, i], ang[:, i], -3.1415925, None, ALU.max))
            g.tensor_copy(ang[:, 2], ang[:, 3]).then_inc(ang_ready, 1)

            pool.wait_ge(rm_sum, upto(rm_sum, 1))
            rstd(rm[:], rm[:], D, 2).then_inc(rm_done, 1)
            for l in range(L):
                pool.wait_ge(kv_sum, upto(kv_sum, l + 1))
                link(rstd(r8[:], sq8[:], HD, 8))
                kv = R2[:].rearrange("p a b -> p (a b)").rearrange("p (n d) -> p n d", d=HD)
                g.tensor_tensor(kv, kv, r8[:].unsqueeze(2).to_broadcast([P, 8, HD]), ALU.mult).then_inc(kv_norm, 1)

            def rope(v, heads, hf, f0):
                n = heads * hf

                def rv(i):
                    return rt[:, i, 0:NT * n].rearrange("p (t h f) -> p t h f", t=NT, h=heads)
                x1, x2 = v[:, :, :, 0:hf], v[:, :, :, hf:2 * hf]
                sn = snc[:, 0, :, f0:f0 + hf].unsqueeze(2).to_broadcast([P, NT, heads, hf])
                cs = snc[:, 1, :, f0:f0 + hf].unsqueeze(2).to_broadcast([P, NT, heads, hf])
                g.tensor_tensor(rv(0), x1, cs, ALU.mult)
                g.tensor_tensor(rv(1), x2, sn, ALU.mult)
                g.tensor_tensor(rv(2), x2, cs, ALU.mult)
                link(g.tensor_tensor(rv(3), x1, sn, ALU.mult))
                g.tensor_tensor(x1, rv(0), rv(1), ALU.subtract)
                return g.tensor_tensor(x2, rv(2), rv(3), ALU.add)

            def heads_view(t, n):
                return t.rearrange("p t (h d) -> p t h d", h=n)

            def unrotate(l, j):
                upto = counter(l)
                pool.wait_ge(scanned, upto(scanned, j + 1))
                if j >= 2:
                    pool.wait_ge(yprod, upto(yprod, j - 1))
                b, jj = divmod(j, TB)
                z = vz[:, j % 2]
                for i in (1, 0):
                    ins = g.tensor_tensor(qq[:, i], z, tab[:, b % 2, i, jj, :].unsqueeze(1).to_broadcast([P, 2, S]),
                                          ALU.mult)
                link(ins)
                g.tensor_tensor(xs[:, j % 2, 0], qq[:, 1, 0], qq[:, 0, 1], ALU.subtract)
                g.tensor_tensor(xs[:, j % 2, 1], qq[:, 0, 0], qq[:, 1, 1], ALU.add).then_inc(unrot, 1)
                pool.wait_ge(unrot, ST * l + j + 1)

            def head_norm(l, n, v):
                upto = counter(l)
                pool.wait_ge(sq_read, upto(sq_read, n + 1))
                link(rstd(r8[:], sq8[:], HD, 8))
                vv = v.rearrange("p t (h d) -> p (t h) d", d=HD)
                return g.tensor_tensor(vv, vv, r8[:].unsqueeze(2).to_broadcast([P, 8, HD]), ALU.mult)

            for l in range(L):
                upto = counter(l)
                for s in range(SLOTS):
                    if s + AHEAD in POOL_LO:
                        n = s + AHEAD
                        pool.wait_ge(hi_done, upto(hi_done, n + 1))
                        g.tensor_tensor(wlo[:, n % RING, :], raw[:, n % RING, :], whi[:, n % RING, :].bitcast(F32),
                                        ALU.subtract).then_inc(lo_pool, 1)
                    if s == 3:
                        pool.wait_ge(rs_sum, upto(rs_sum, 1))
                        link(rstd(rs[:], rs[:], D, 2))
                        g.tensor_scalar(rsh[:], rs[:], 0.5, None, ALU.mult).then_inc(rs_done, 1)
                    if s - 1 in BU:
                        unrotate(l, BU[s - 1])
                    if s in (16, 24):
                        i = s // 8 - 2
                        pool.wait_ge(taken, upto(taken, G_IQ0 + i + 1))
                        if l == 0:
                            pool.wait_ge(rope_ready, counter(None)(rope_ready, 1))
                        rope(heads_view(iq[:, :, i * 512:(i + 1) * 512], 8), 8, 8, 0).then_inc(roped_iq, 1)
                        pool.wait_ge(roped_iq, upto(roped_iq, i + 1))
                    if s == 32:
                        pool.wait_ge(taken, upto(taken, G_MISC + 1))
                        ik = misc[:, :, MISC["ik"]:MISC["ik"] + ID]
                        link(rope(heads_view(ik, 1), 1, 8, 0))
                        pool.wait_ge(k_sum, upto(k_sum, 1))
                        for i in range(2):
                            g.tensor_copy(ikd[:, :, i * ID:(i + 1) * ID], ik)
                        iw = misc[:, :, MISC["iw"]:MISC["iw"] + IH]
                        link(g.tensor_scalar(iw, iw, IH ** -0.5 * ID ** -0.5, None, ALU.mult))
                        link(rstd(rk[:], sqk[:], HD, 2))
                        k = misc[:, :, 0:HD]
                        link(g.tensor_tensor(k, k, rk[:].unsqueeze(2).to_broadcast([P, NT, HD]), ALU.mult))
                        kg = pa[:, PC["kg"]:PC["kg"] + HD].unsqueeze(1).to_broadcast([P, NT, HD])
                        link(g.tensor_tensor(k, k, kg, ALU.mult))
                        rope(heads_view(k, 1), 1, 16, 8).then_inc(roped_k, 1)
                        pool.wait_ge(roped_k, upto(roped_k, 1))
                    if s == 41:
                        head_norm(l, SQ_DQ, E1[:]).then_inc(normr, 1)
                        pool.wait_ge(normr, upto(normr, 1))
                        qv = E1[:].rearrange("p t (h d) -> p (t h) d", d=HD)
                        qg = pa[:, PC["qg"]:PC["qg"] + HD].unsqueeze(1).to_broadcast([P, 8, HD])
                        link(g.tensor_tensor(qv, qv, qg, ALU.mult))
                        rope(heads_view(E1[:], H), H, 16, 8).then_inc(roped_q, 1)
                        pool.wait_ge(roped_q, upto(roped_q, 1))
                    for n, v in ((SQ_DSA, obuf[:, B_DSA]), (SQ_MQ, E2[:]), (SQ_GLA, obuf[:, B_GLA]),
                                 (SQ_S5, obuf[:, B_S5]), (SQ_MEM, obuf[:, B_MEM])):
                        if s == NORM_SLOT[n]:
                            head_norm(l, n, v).then_inc(normr, 1)
                            pool.wait_ge(normr, upto(normr, n + 1))

        @block.tensor
        def _(pe):
            mm = nc.tensor.matmul
            plink = linker(pe, pe_own)
            tr = nc.tensor.transpose

            def slot_products(n, l, g, c, hi, lo, width):
                final = l == L - 1 and n == SLOTS - 1
                pe.wait_ge(*low_part(l, n))
                for a in range(CK):
                    for b in range(NT):
                        kk, t = (b, a) if final else (a, b)
                        k = CK * c + kk
                        o = acc[g % 2][t][:, 0:width]
                        h_, l_ = hi[:, k, t * P:(t + 1) * P], lo[:, k, t * P:(t + 1) * P]
                        wh = whi[:, n % RING, kk * W:kk * W + width]
                        wl = wlo[:, n % RING, kk * W:kk * W + width]
                        mm(o, h_, wh, start=(k == 0), stop=False)
                        mm(o, h_, wl, start=False, stop=False)
                        last = mm(o, l_, wh, start=False, stop=(k == KT - 1))
                    if final and a == 0:
                        last.then_inc(tile_done, 1)
                last.then_inc(used, 1)

            def memory_turn(c):
                if c >= 2:
                    pe.wait_ge(freeB, counter(None)(freeB, c - 1))
                if c % 2 == 0:
                    pe.wait_ge(mem_in[c // 2], 16)
                bank = memory_bank(c)
                for kk in range(CK):
                    for t in range(NT):
                        last = tr(bank[:, (kk * NT + t) * P:(kk * NT + t + 1) * P],
                                  memr[:, t, (CK * c + kk) * P:(CK * c + kk + 1) * P], ident[:])
                last.then_inc(wroteB, 1)

            def turn(l, index, src, c):
                upto = counter(l)
                pe.wait_ge(freeB, upto(freeB, index))
                for kk in range(CK):
                    for t in range(NT):
                        last = tr(bankB[:, (kk * NT + t) * P:(kk * NT + t + 1) * P],
                                  src[:, t, kk * P:(kk + 1) * P], ident[:])
                last.then_inc(wroteB, 1)

            upto = counter(None)
            pe.wait_ge(ident_ready, upto(ident_ready, 1))
            memory_turn(0)
            memory_turn(1)
            for n in range(PRO):
                g, c = divmod(n, NC)
                if n == SQUARE_P[0]:
                    pe.wait_ge(consts, upto(consts, 1))
                if n in TURN_P:
                    i = TURN_P[n]
                    pe.wait_ge(x_in, upto(x_in, 48))
                    turn(None, NC + i, xr[:, i // 2, :, (i % 2) * 256:(i % 2 + 1) * 256], i)
                if n in KV_TURN:
                    ml = KV_TURN[n]
                    for i in range(2):
                        k = 2 * ml + i
                        if ml >= 1:
                            pe.wait_ge(freeA[i], upto(freeA[i], k // 2))
                        pe.wait_ge(kv_norm, upto(kv_norm, ml + 1))
                        for hh in range(2):
                            for t in range(NT):
                                last = tr(bankA[i][:, (hh * NT + t) * P:(hh * NT + t + 1) * P],
                                          R2[:].rearrange("p a b -> p (a b)").rearrange("p (t d) -> p t d", t=NT)[
                                              :, t, (2 * i + hh) * P:(2 * i + hh + 1) * P], ident[:])
                        last.then_inc(stepped, 1)
                if c == 0 and g >= 2:
                    pe.wait_ge(taken, upto(taken, g - 1))
                if g == 0:
                    pe.wait_ge(freeB, upto(freeB, c + 1))
                hi, lo = (hhi, hlo) if g < 2 else (mhi, mlo)
                if n + 2 < NC:
                    memory_turn(n + 2)
                slot_products(n, None, g, c, hi, lo, W)

            def step(l, name):
                upto = counter(l)
                n = NUM[name]
                b = bank_of(name)
                pe.wait_ge(freeA[n % 2], upto(freeA[n % 2], n // 2))

                def q(i, w=P):
                    return b[:, i * w:(i + 1) * w]

                def tok(t):
                    return slice(t * P, (t + 1) * P)
                if name in ("iqT0", "iqT1", "iqT2", "iqT3"):
                    i = int(name[-1])
                    pe.wait_ge(roped_iq, upto(roped_iq, i // 2 + 1))
                    for pp in range(2):
                        for t in range(NT):
                            last = tr(q(pp * NT + t), iq[:, t, (2 * i + pp) * P:(2 * i + pp + 1) * P], ident[:])
                elif name == "ikT":
                    pe.wait_ge(roped_k, upto(roped_k, 1))
                    for t in range(NT):
                        tr(q(t), ikd[:, t, :], ident[:])
                    for t in range(NT):
                        last = tr(q(2 + t), misc[:, t, 0:HD], ident[:])
                elif name == "glrT":
                    for t in range(NT):
                        last = tr(b[0:16, tok(t)], misc[:, t, MISC["glr"]:MISC["glr"] + 16], ident[:])
                elif name == "gate":
                    pe.wait_ge(*result(upto, "glrT"))
                    pe.wait_ge(par_in, upto(par_in, 64))
                    for t in range(NT):
                        last = mm(q(t, S), t1[0:16, 0, tok(t)], wu[:], start=True, stop=True)
                elif name in ("uT0", "uT1"):
                    i = int(name[-1])
                    pe.wait_ge(taken, upto(taken, G_SU + 1))
                    for cc in range(2):
                        for t in range(NT):
                            last = tr(q(cc * NT + t), E1[:, t, (2 * i + cc) * P:(2 * i + cc + 1) * P], ident[:])
                elif name.startswith("rel1"):
                    i = int(name[-1])
                    pe.wait_ge(*result(upto, "iqT3"))
                    pe.wait_ge(*result(upto, "ikT"))
                    r = slice(ID * (i % 2), ID * (i % 2) + ID)
                    for hh in range(2):
                        last = mm(q(hh, S), iqT[r, i // 2 * 2 + hh, P:S], kkT[r, 0, :], start=True, stop=True)
                elif name.startswith("rel0"):
                    i = int(name[-1])
                    r = slice(ID * (i % 2), ID * (i % 2) + ID)
                    for hh in range(4):
                        last = mm(q(hh), iqT[r, i // 2 * 4 + hh, 0:P], kkT[r, 0, 0:P], start=True, stop=True)
                elif name in ("qT0", "qT1"):
                    i = int(name[-1])
                    pe.wait_ge(roped_q, upto(roped_q, 1))
                    for hh in range(2):
                        for t in range(NT):
                            last = tr(q(hh * NT + t), E1[:, t, (2 * i + hh) * P:(2 * i + hh + 1) * P], ident[:])
                elif name.startswith("lg1"):
                    i = int(name[-1])
                    pe.wait_ge(*result(upto, "qT0"))
                    pe.wait_ge(*result(upto, "qT1"))
                    for hh in range(2):
                        last = mm(q(hh, S), qT[:, 2 * i + hh, P:S], kkT[:, 1, :], start=True, stop=True)
                elif name == "lg0":
                    for hh in range(H):
                        last = mm(q(hh), qT[:, hh, 0:P], kkT[:, 1, 0:P], start=True, stop=True)
                elif name in ("cumD", "cumT", "cumL"):
                    pe.wait_ge(lsum, upto(lsum, 1))
                    m = {"cumD": triM, "cumT": tri, "cumL": triL}[name]
                    for t in range(NT):
                        last = mm(q(t, S), m[:], la[:, t, :], start=True, stop=True)
                elif name == "dec":
                    for hp in range(2):
                        for t in range(NT):
                            last = mm(b[:, hp * 4 + t * 2:hp * 4 + t * 2 + 2], la[:, t, hp * P:(hp + 1) * P], cind[:],
                                      start=True, stop=True)
                elif name.startswith("pT1"):
                    i = int(name[-1])
                    pe.wait_ge(exp1, upto(exp1, 1))
                    for hh in range(2):
                        for t in range(NT):
                            last = tr(q(hh * NT + t), P1[:, 2 * i + hh, tok(t)], ident[:])
                elif name == "pT0":
                    pe.wait_ge(exp0, upto(exp0, 1))
                    for hh in range(H):
                        last = tr(q(hh), P0[:, hh, :], ident[:])
                elif name == "pv1":
                    pe.wait_ge(*result(upto, "pT1_0"))
                    pe.wait_ge(*result(upto, "pT1_1"))
                    for hh in range(H):
                        for t in range(NT):
                            last = mm(q(hh), pT[:, hh, t, :], misc[:, t, HD:2 * HD], start=(t == 0), stop=(t == 1))
                elif name == "pv0":
                    pe.wait_ge(*result(upto, "pT0"))
                    for hh in range(H):
                        last = mm(q(hh), pT[:, hh, 0, :], misc[:, 0, HD:2 * HD], start=True, stop=True)
                elif name in ("qeT", "keT", "qbT"):
                    src = {"qeT": t1, "keT": t2, "qbT": t3}[name]
                    pe.wait_ge(gmul, upto(gmul, {"qeT": 1, "keT": 1, "qbT": 2}[name]))
                    for hp in range(2):
                        for t in range(NT):
                            last = tr(q(hp * NT + t), src[:, t, hp * P:(hp + 1) * P], ident[:])
                elif name in ("at0", "at1"):
                    t = int(name[-1])
                    pe.wait_ge(*result(upto, "qeT"))
                    pe.wait_ge(*result(upto, "keT"))
                    for hh in (0, 2, 1, 3):
                        r = slice(GD * (hh % 2), GD * (hh % 2) + GD)
                        last = mm(q(hh), keT[r, hh // 2, tok(t)], qeT[r, hh // 2, tok(t)], start=True, stop=True)
                        if hh == 2:
                            plink(last)
                elif name in ("dS0", "dS1"):
                    pe.wait_ge(gmul, upto(gmul, 3))
                    pe.wait_ge(taken, upto(taken, G_GV + 1))
                    for i, ch in enumerate((0, 1) if name == "dS0" else (2,)):
                        r = slice(GD * (ch % 2), GD * (ch % 2) + GD)
                        for hh in range(H):
                            o = b[GD * (hh % 2):GD * (hh % 2) + GD, (2 * i + hh // 2) * P:(2 * i + hh // 2 + 1) * P]
                            last = mm(o, kd[r, ch // 2, hh * GD:(hh + 1) * GD], E1[r, ch // 2, hh * P:(hh + 1) * P],
                                      start=True, stop=True)
                        if ch == 0:
                            plink(last)
                elif name in ("go0", "go1"):
                    t = int(name[-1])
                    pe.wait_ge(*result(upto, f"at{t}"))
                    pe.wait_ge(*result(upto, "dS0"))
                    pe.wait_ge(*result(upto, "dS1"))
                    pe.wait_ge(*result(upto, "qbT"))
                    for hh in range(H):
                        last = mm(q(hh), attn[:, hh, :], E1[:, t, hh * P:(hh + 1) * P], start=(hh == 0),
                                  stop=False, skip_group_check=True)
                    plink(last)
                    for hh in (0, 2, 1, 3):
                        r = slice(GD * (hh % 2), GD * (hh % 2) + GD)
                        for cc in range(2):
                            ch = 2 * t + cc
                            if ch > 0:
                                last = mm(b[GD * cc:GD * cc + GD, hh * P:(hh + 1) * P],
                                          qbT[r, hh // 2, ch * GD:(ch + 1) * GD], stt_[r, ch - 1, hh // 2, :],
                                          start=False, stop=True, skip_group_check=True)
                        if hh == 2:
                            plink(last)
                elif name in ("mqT0", "mqT1"):
                    i = int(name[-1])
                    pe.wait_ge(normr, upto(normr, SQ_MQ + 1))
                    for hh in range(2):
                        for t in range(NT):
                            last = tr(q(hh * NT + t), E2[:, t, (2 * i + hh) * P:(2 * i + hh + 1) * P], ident[:])
                elif name[:2] == "ml":
                    t, i = int(name[2]), int(name[4])
                    pe.wait_ge(*result(upto, "mqT0"))
                    pe.wait_ge(*result(upto, "mqT1"))
                    pe.wait_ge(mk_in, upto(mk_in, 16))
                    for hh in range(2):
                        last = mm(q(hh, S), mqT[:, 2 * i + hh, tok(t)], mkT[:, 2 * i + hh, :], start=True, stop=True)
                elif name[:2] == "mp":
                    t, i = int(name[2]), int(name[4])
                    pe.wait_ge(*result(upto, f"ml{t}_0"))
                    pe.wait_ge(*result(upto, f"ml{t}_1"))
                    for hh in range(2):
                        for st in range(NT):
                            last = tr(q(hh * NT + st), Pm[:, 2 * i + hh, tok(st)], ident[:])
                elif name[:2] == "mv":
                    t = int(name[2])
                    pe.wait_ge(*result(upto, f"mp{t}_0"))
                    pe.wait_ge(*result(upto, f"mp{t}_1"))
                    pe.wait_ge(mv_in, upto(mv_in, 16))
                    for hh in range(H):
                        for st in range(NT):
                            last = mm(q(hh), pT[:, hh, st, :], mv[:, st, hh * P:(hh + 1) * P],
                                      start=(st == 0), stop=(st == 1))
                elif name[:2] == "yt":
                    t = int(name[2])
                    pe.wait_ge(gelud, upto(gelud, 4))
                    for ct in range(4):
                        last = tr(q(ct), ych[:, ct, tok(t)], ident[:])
                elif name[:3] == "glu":
                    t = int(name[3])
                    pe.wait_ge(glu_in, upto(glu_in, 16))
                    for ct in range(4):
                        last = mm(b[:], ych[:, ct, tok(t)], wg[:, ct, :], start=(ct == 0), stop=(ct == 3))
                last.then_inc(stepped, 1)

            for l in range(L):
                upto = counter(l)
                for s in range(SLOTS):
                    g, c = divmod(s, NC)
                    if s in AT:
                        step(l, AT[s])
                    if s in TURN_X:
                        if l == 0:
                            pe.wait_ge(x_in, upto(x_in, 0))
                        else:
                            pe.wait_ge(added, upto(added, 0))
                        cx = TURN_X[s]
                        turn(l, BX + s - 2, xr[:, 0, :, (cx % 2) * 256:(cx % 2 + 1) * 256], cx)
                    if s in BU:
                        j = BU[s]
                        ct, jj = divmod(j, 4)
                        pe.wait_ge(freeB, upto(freeB, BBU + j))
                        if j == 0:
                            pe.wait_ge(par_in, upto(par_in, 64))
                            pe.wait_ge(*result(upto, "uT0"))
                            pe.wait_ge(*result(upto, "uT1"))
                        r = slice(32 * jj, 32 * jj + 32)
                        for i in range(2):
                            last = mm(bankB[:, i * S:(i + 1) * S], bm[r, ct, i, :], uT[r, ct, :], start=True, stop=True)
                        last.then_inc(wroteB, 1)
                    if s in YS:
                        j = YS[s]
                        ct, jj = divmod(j, 4)
                        pe.wait_ge(unrot, upto(unrot, j + 1))
                        if j == 0:
                            pe.wait_ge(s5_c, upto(s5_c, 1))
                        if jj == 0 and l + ct >= 1:
                            pe.wait_ge(ypoly, upto(ypoly, ct))
                        r = slice(32 * jj, 32 * jj + 32)
                        o = bankY[r, ct % 2, :]
                        mm(o, cp[:, j, 0, :], xs[:, j % 2, 0], start=True, stop=False, skip_group_check=True)
                        mm(o, cp[:, j, 1, :], xs[:, j % 2, 1], start=False, stop=True,
                           skip_group_check=True).then_inc(yprod, 1)
                    if s in TURN_O:
                        co = TURN_O[s]
                        pe.wait_ge(zmul, upto(zmul, co // 2 + 1))
                        turn(l, BO + co, obuf[:, co // 2, :, (co % 2) * 256:(co % 2 + 1) * 256], co)
                    if s in TURN_N and l + 1 < L:
                        cn = TURN_N[s]
                        pe.wait_ge(added, upto(added, cn // 2 + 1))
                        turn(l, BN + cn, xr[:, cn // 2, :, (cn % 2) * 256:(cn % 2 + 1) * 256], cn)
                    if c == 0:
                        if g < 2:
                            if l == 0:
                                pe.wait_ge(taken, upto(taken, g - 1))
                            else:
                                pe.wait_ge(added, upto(added, g - 1))
                        elif g - 2 < 8:
                            pe.wait_ge(taken, upto(taken, g - 1))
                        elif g - 2 < 12:
                            pe.wait_ge(gated, upto(gated, g - 2 - 8 + 1))
                        else:
                            pe.wait_ge(added, upto(added, g - 2 - 12 + 1))
                    if g == 0:
                        if c < 6:
                            pe.wait_ge(freeB, upto(freeB, c - 6 + 1))
                        else:
                            pe.wait_ge(freeB, upto(freeB, BX + c - 6 + 1))
                    if g == G_OUT:
                        pe.wait_ge(freeB, upto(freeB, BO + c + 1))
                    slot_products(s, l, g, c, hhi, hlo, MISC["end"] if g == G_MISC else W)

        @block.scalar
        def _(act):
            link = linker(act, act_own)
            fn = nc.scalar.activation
            R2f = R2[:].rearrange("p a b -> p (a b)")

            def split_hi(n, l):
                upto = counter(l)
                act.wait_ge(landed[n % RING], upto(landed[n % RING], 16 * (n // RING + 1)))
                if l is not None or n >= RING:
                    act.wait_ge(used, upto(used, n - RING + 1))
                fn(whi[:, n % RING, :], raw[:, n % RING, :], ACT.Copy).then_inc(hi_done, 1)

            def turn_hi(l, index, dst, gain, c, free_at):
                upto = counter(l)
                act.wait_ge(wroteB, upto(wroteB, index + 1))
                if free_at is not None:
                    act.wait_ge(used, upto(used, free_at))
                for kk in range(CK):
                    k = CK * c + kk
                    ins = fn(dst[:, k, :], bankB[:, kk * S:(kk + 1) * S], ACT.Copy, scale=gain(k))
                ins.then_inc(turned_hi, 1)

            def square_piece(b, g):
                for t in range(NT):
                    ins = fn(E3[:, t, :], xr[:, b, t, :], ACT.Square, accum_out=ssx[:, t, g:g + 1])
                ins.then_inc(sq_x, 1)

            def copy(name, dst, **kw):
                fn(dst, bank_of(name)[:], ACT.Copy, **kw).then_inc(freeA[NUM[name] % 2], 1)

            upto = counter(None)
            def memory_hi(c):
                act.wait_ge(wroteB, upto(wroteB, c + 1))
                for l, dst in enumerate((hhi, mhi)):
                    for kk in range(CK):
                        k = CK * c + kk
                        ins = fn(dst[:, k, :], memory_bank(c)[:, kk * S:(kk + 1) * S], ACT.Copy, scale=mg[:, l, k:k + 1])
                ins.then_inc(turned_hi, 1)

            act.wait_ge(ident_ready, upto(ident_ready, 1))
            fn(warm[:], ident[:, 0:1], ACT.Copy)
            act.wait_ge(mg_in, upto(mg_in, 16))
            memory_hi(0)
            split_hi(0, None)
            for n in range(PRO):
                if n + 1 < NC:
                    memory_hi(n + 1)
                if n == 0:
                    for k in range(1, AHEAD):
                        split_hi(k, None)
                if n in TURN_P:
                    if TURN_P[n] == 0:
                        act.wait_ge(par_in, upto(par_in, 64))
                    turn_hi(None, NC + TURN_P[n], hhi, lambda k: col("ln", k), TURN_P[n], NC + TURN_P[n] + 1)
                if n == 1:
                    split_hi(AHEAD, None)
                if 1 <= n < PRO - AHEAD:
                    split_hi(n + AHEAD, None)
                elif n > 0:
                    split_hi(n + AHEAD - PRO, 0)
                if n in MEM_SQUARE:
                    t, i = divmod(n - MEM_SQUARE[0], 4)
                    act.wait_ge(mem_in[i], upto(mem_in[i], 16))
                    link(fn(R2f[:, 0:W], memr[:, t, i * W:(i + 1) * W], ACT.Square, accum_out=ssm[:, t, i:i + 1]))
                    if n == MEM_SQUARE[-1]:
                        fn(R2f[:, 0:8], ssm[:].rearrange("p a b -> p (a b)"), ACT.Copy).then_inc(sq_mem, 1)
                if n == 18:
                    act.wait_ge(ang_ready, upto(ang_ready, 1))
                    for i in range(2):
                        ins = fn(snc[:, i], ang[:, i], ACT.Sin)
                    ins.then_inc(rope_ready, 1)
                if n in KV_COPY:
                    ml = KV_COPY[n]
                    act.wait_ge(used, upto(used, 16 * ml + NC))
                    act.wait_ge(rm_done, upto(rm_done, 1))
                    if ml == 1:
                        act.wait_ge(k_out[0], 16)
                    for t in range(NT):
                        ins = fn(R2f[:, t * W:(t + 1) * W], acc[0][t][:], ACT.Copy, scale=rm[:, t:t + 1])
                    ins.then_inc(taken, 1)
                    act.wait_ge(taken, upto(taken, 2 * ml + 1))
                    fn(kvT[:].rearrange("p a b -> p (a b)"), R2f, ACT.Square).then_inc(sq_kv, 1)
                if n in KV_READ:
                    ml = KV_READ[n]
                    for i in range(2):
                        act.wait_ge(stepped, upto(stepped, 2 * ml + 2))
                        fn(kvT[:, 2 * i:2 * i + 2, :].rearrange("p a b -> p (a b)"), bankA[i][:], ACT.Copy,
                           scale=mg[:, ml, MG["mk"]:MG["mk"] + 1]).then_inc(freeA[i], 1)
                if n == 16:
                    act.wait_ge(used, upto(used, 16))
                    for t in range(NT):
                        ins = fn(R1[:, t, :], acc[1][t][:], ACT.Copy, scale=rm[:, t:t + 1])
                    ins.then_inc(taken, 1)
                if n in SQUARE_P:
                    i = SQUARE_P.index(n)
                    act.wait_ge(x_in, upto(x_in, 48))
                    if i >= 1:
                        act.wait_ge(sq_x, upto(sq_x, i))
                    square_piece(i, i)

            dst_of = {G_IQ0: iq[:, :, 0:W], G_IQ1: iq[:, :, W:2 * W], G_MISC: misc[:], G_SU: E1[:], G_DQ: E1[:],
                      G_GQK: E2[:], G_GV: E1[:], G_MQ: E2[:]}
            for l in range(L):
                upto = counter(l)
                for s in range(SLOTS):
                    g, c = divmod(s, NC)
                    if s in TURN_X:
                        cx = TURN_X[s]
                        turn_hi(l, BX + s - 2, hhi, lambda k: col("ln", k), cx,
                                NC + cx + 1 - PRO if l == 0 else (GROUPS - 1) * NC + cx + 1 - SLOTS)
                    if s in TURN_O:
                        co = TURN_O[s]
                        turn_hi(l, BO + co, hhi, lambda k: col("on", k), co, (G_OUT - 1) * NC + co + 1)
                    if s in TURN_N and l + 1 < L:
                        cn = TURN_N[s]
                        act.wait_ge(par_in, upto(par_in, 128))
                        turn_hi(l, BN + cn, hhi, lambda k: col("ln", k), cn, (GROUPS - 1) * NC + cn + 1)
                    if s + AHEAD < SLOTS:
                        split_hi(s + AHEAD, l)
                    elif l + 1 < L:
                        split_hi(s + AHEAD - SLOTS, l + 1)
                    if s == 0 and l == 0:
                        act.wait_ge(used, counter(None)(used, PRO))
                        act.wait_ge(v_out[0], 16)
                        for t in range(NT):
                            ins = fn(R1[:, t, :], acc[1][t][:], ACT.Copy, scale=rm[:, t:t + 1])
                        ins.then_inc(taken, 1)
                    if s == 1:
                        if l == 0:
                            act.wait_ge(x_in, upto(x_in, 0))
                        else:
                            act.wait_ge(added, upto(added, 0))
                        square_piece(0, 3)
                    if s == 2:
                        if l == 0:
                            act.wait_ge(par_in, counter(l)(par_in, 64))
                        fn(s5[:, 0, :], pa[:, PC["lst"]:PC["lst"] + ST], ACT.Exp).then_inc(s5_exp, 1)
                    if s == 5:
                        act.wait_ge(s5_phase, upto(s5_phase, 1))
                        fn(s5[:, 5, :], s5[:, 1, :], ACT.Exp)
                        fn(s5[:, 6, :], s5[:, 4, :], ACT.Sin, scale=TURN / 2)
                        fn(s5[:, 7, :], s5[:, 4, :], ACT.Sin, scale=TURN).then_inc(s5_sin, 1)
                    if s in SIN_SLOT:
                        b = SIN_SLOT.index(s)
                        act.wait_ge(frac, upto(frac, b + 1))
                        link(fn(tab[:, b % 2, 1], tab[:, b % 2, 0], ACT.Abs))
                        fn(tab[:, b % 2, 0], tab[:, b % 2, 0], ACT.Sin, scale=TURN)
                        fn(tab[:, b % 2, 1], tab[:, b % 2, 1], ACT.Sin, scale=-TWO_PI,
                           bias=quarter[:]).then_inc(phased, 1)
                    if c == 0 and 1 <= g <= G_Z:
                        act.wait_ge(used, upto(used, NC * g))
                        if g == 1:
                            act.wait_ge(rs_done, upto(rs_done, 1))
                            if l == 0:
                                act.wait_ge(used, counter(None)(used, PRO))
                            else:
                                act.wait_ge(freeB, counter(l - 1)(freeB, BO + 8))
                        if g - 1 == G_DQ:
                            act.wait_ge(stepped, upto(stepped, NUM["uT1"] + 1))
                        if g - 1 == G_GV:
                            act.wait_ge(stepped, upto(stepped, NUM["qT1"] + 1))
                        if g - 1 == G_MQ:
                            act.wait_ge(gmul, upto(gmul, 3))
                        w = MISC["end"] if g - 1 == G_MISC else W
                        for t in range(NT):
                            ins = fn(dst_of[g - 1][:, t, :], acc[(g - 1) % 2][t][:, 0:w], ACT.Copy,
                                     scale=rs[:, t:t + 1])
                        ins.then_inc(taken, 1)
                    if s == NC * (G_MISC + 1):
                        act.wait_ge(taken, upto(taken, G_MISC + 1))
                        act.wait_ge(stepped, upto(stepped, NUM["iqT3"] + 1))
                        for t in range(NT):
                            ins = fn(ikd[:, t, :], misc[:, t, 0:HD], ACT.Square, accum_out=sqk[:, t:t + 1])
                        ins.then_inc(k_sum, 1)
                    if c == 0 and G_Z < g <= G_OUT:
                        z = g - G_Z - 1
                        act.wait_ge(used, upto(used, NC * g))
                        if l + z >= 1:
                            act.wait_ge(zmul, upto(zmul, z))
                        if z == 0:
                            act.wait_ge(stepped, upto(stepped, NUM["dec"] + 1))
                        for t in range(NT):
                            ins = fn(Ez[:, t, :], acc[(g - 1) % 2][t][:], ACT.Tanh, scale=rsh[:, t:t + 1])
                        ins.then_inc(ztanh, 1)
                    if s in (105, 113, 121) and l + 1 < L:
                        g_ = (s - 105) // 8
                        act.wait_ge(added, upto(added, g_ + 1))
                        square_piece(g_, g_)
                    for n, src in enumerate((E1, E2, None, None, None, None)):
                        if s != NORM_SLOT[n]:
                            continue
                        if l + n >= 1:
                            act.wait_ge(sq_read, upto(sq_read, n))
                        if n == SQ_DQ:
                            act.wait_ge(taken, upto(taken, G_DQ + 1))
                        if n == SQ_MQ:
                            act.wait_ge(taken, upto(taken, G_MQ + 1))
                        if n == SQ_DSA:
                            act.wait_ge(*result(upto, "pv1"))
                            act.wait_ge(*result(upto, "pv0"))
                        if n == SQ_GLA:
                            act.wait_ge(*result(upto, "go1"))
                        if n == SQ_MEM:
                            act.wait_ge(*result(upto, "mv0"))
                            act.wait_ge(*result(upto, "mv1"))
                        if n == SQ_S5:
                            act.wait_ge(obr, upto(obr, 1))
                        b = {SQ_DSA: B_DSA, SQ_GLA: B_GLA, SQ_MEM: B_MEM, SQ_S5: B_S5}.get(n)
                        v = src[:] if src is not None else obuf[:, b]
                        fn(E3[:], v, ACT.Square).then_inc(squared, 1)
                    if s in AT:
                        name = AT[s]
                        n = NUM[name]
                        b = bank_of(name)
                        fa = freeA[n % 2]
                        if name not in ("gate", "lg1_0", "lg1_1", "lg0", "pv1", "pv0", "at0", "at1", "dS0", "dS1",
                                        "go0", "go1", "mv0", "mv1"):
                            act.wait_ge(stepped, upto(stepped, n + 1))
                        if name[:3] == "iqT":
                            i = int(name[-1])
                            copy(name, iqT[:, 2 * i:2 * i + 2, :].rearrange("p a b -> p (a b)"))
                        elif name == "ikT":
                            copy(name, kkT[:].rearrange("p a b -> p (a b)"))
                        elif name == "glrT":
                            fn(t1[0:16, 0, :], b[0:16, 0:S], ACT.Copy).then_inc(fa, 1)
                        elif name in ("uT0", "uT1"):
                            i = int(name[-1])
                            copy(name, uT[:, 2 * i:2 * i + 2, :].rearrange("p a b -> p (a b)"))
                        elif name[:3] == "rel":
                            i = n - NUM["rel1_0"]
                            if l == 0 and i == 0:
                                act.wait_ge(v_out[1], 16)
                            if i >= 2:
                                act.wait_ge(weighed, upto(weighed, i - 1))
                            fn(rel[:, i % 2, :], b[:], ACT.Relu).then_inc(fa, 1)
                        elif name in ("qT0", "qT1"):
                            i = int(name[-1])
                            copy(name, qT[:, 2 * i:2 * i + 2, :].rearrange("p a b -> p (a b)"))
                        elif name == "cumD":
                            bb = b[:].rearrange("p (t d) -> p t d", t=NT)
                            fn(t1[:], bb, ACT.Exp, scale=1.0 / 16)
                            fn(t2[:], bb, ACT.Exp, scale=-1.0 / 16).then_inc(fa, 1)
                        elif name in ("cumT", "cumL"):
                            fn((t3 if name == "cumT" else kd)[:], b[:].rearrange("p (t d) -> p t d", t=NT), ACT.Exp,
                               scale=1.0 / 16).then_inc(fa, 1)
                        elif name == "dec":
                            fn(dec[:], b[:, 0:8].rearrange("p (a c) -> p a c", a=2), ACT.Exp, scale=1.0 / 16).then_inc(fa, 1)
                        elif name[:3] == "pT1":
                            i = int(name[-1])
                            copy(name, pT[:, 2 * i:2 * i + 2].rearrange("p a b c -> p (a b c)"))
                        elif name == "pT0":
                            act.wait_ge(stepped, upto(stepped, NUM["pv1"] + 1))
                            fn(pT[:, :, 0, :], b[:].rearrange("p (h t) -> p h t", h=H), ACT.Copy).then_inc(fa, 1)
                        elif name in ("qeT", "keT", "qbT"):
                            copy(name, {"qeT": qeT, "keT": keT, "qbT": qbT}[name][:].rearrange("p a b -> p (a b)"))
                        elif name in ("mqT0", "mqT1"):
                            i = int(name[-1])
                            copy(name, mqT[:, 2 * i:2 * i + 2, :].rearrange("p a b -> p (a b)"), scale=col("mqg"))
                        elif name[:2] == "ml":
                            t, i = int(name[2]), int(name[4])
                            act.wait_ge(mmax, upto(mmax, 2 * t + i + 1))
                            if t == 1 and i == 0:
                                act.wait_ge(stepped, upto(stepped, NUM["mp0_1"] + 1))
                            for hh in range(2):
                                h_ = 2 * i + hh
                                ins = fn(Pm[:, h_, :], b[:, hh * S:(hh + 1) * S], ACT.Exp, scale=SCALE,
                                         bias=(nm0, nm1)[t][:, h_:h_ + 1], accum_out=(su0, su1)[t][:, h_:h_ + 1])
                            ins.then_inc(fa, 1)
                        elif name[:2] == "mp":
                            t, i = int(name[2]), int(name[4])
                            if t == 1 and i == 0:
                                act.wait_ge(stepped, upto(stepped, NUM["mv0"] + 1))
                            copy(name, pT[:, 2 * i:2 * i + 2].rearrange("p a b c -> p (a b c)"))
                        elif name[:2] == "yt":
                            t = int(name[2])
                            copy(name, obuf[:, B_S5, t, :], scale=0.25)
                        elif name[:3] == "glu":
                            fn(gt[:, int(name[3]), :], b[:], ACT.Tanh, scale=0.25).then_inc(fa, 1)
                    if s == 40:
                        act.wait_ge(*result(upto, "gate"))
                        link(fn(t1[:], la[:], ACT.Abs))
                        link(fn(t1[:], t1[:], ACT.Exp, scale=-1.0))
                        fn(t1[:], t1[:], ACT.Ln, bias=1.0).then_inc(lsoft, 1)
                    if s == 62:
                        act.wait_ge(biased1, upto(biased1, 1))
                        for hh in range(H):
                            ins = fn(P1[:, hh, :], P1[:, hh, :], ACT.Exp, bias=nm1[:, hh:hh + 1],
                                     accum_out=su1[:, hh:hh + 1])
                        ins.then_inc(exp1, 1)
                    if s == 63:
                        act.wait_ge(biased0, upto(biased0, 1))
                        for hh in range(H):
                            ins = fn(P0[:, hh, :], P0[:, hh, :], ACT.Exp, bias=nm0[:, hh:hh + 1],
                                     accum_out=su0[:, hh:hh + 1])
                        ins.then_inc(exp0, 1)
                    for ct in range(4):
                        if s == S5_SLOT[4 * ct + 3] + S5_LAG + 1:
                            act.wait_ge(ypoly, upto(ypoly, ct + 1))
                            fn(ytmp[:], ytmp[:], ACT.Tanh, scale=GELU_CUBE * math.sqrt(2 / math.pi)).then_inc(ytanh, 1)

        @block.vector
        def _(dve):
            link = linker(dve, dve_own)
            v_ = nc.vector

            def split_lo(n, l):
                upto = counter(l)
                dve.wait_ge(hi_done, upto(hi_done, n + 1))
                v_.tensor_tensor(wlo[:, n % RING, :], raw[:, n % RING, :], whi[:, n % RING, :].bitcast(F32),
                                 ALU.subtract).then_inc(lo_done, 1)

            def turn_lo(l, index, count, hi, lo, gain, c):
                upto = counter(l)
                dve.wait_ge(turned_hi, upto(turned_hi, count))
                for kk in range(CK):
                    k = CK * c + kk
                    ins = v_.scalar_tensor_tensor(out=lo[:, k, :], in0=bankB[:, kk * S:(kk + 1) * S], scalar=gain(k),
                                                  in1=hi[:, k, :].bitcast(F32), op0=ALU.mult, op1=ALU.subtract)
                ins.then_inc(freeB, 1)

            def x_add(l, g):
                upto = counter(l)
                dve.wait_ge(used, upto(used, (G_OUT + g + 1) * NC))
                dve.wait_ge(x_in, upto(x_in, 48 if g < 3 else 64))
                for t in range(NT):
                    ins = v_.tensor_tensor(xr[:, g % XB, t, :], acc[g % 2][t][:], xr[:, g % XB, t, :], ALU.add)
                ins.then_inc(added, 1)

            def sum8(dst, src, n):
                return v_.tensor_reduce(dst, src, AX.X, ALU.add)

            upto = counter(None)
            def memory_lo(c):
                dve.wait_ge(turned_hi, upto(turned_hi, c + 1))
                for l, (hi, lo) in enumerate(((hhi, hlo), (mhi, mlo))):
                    for kk in range(CK):
                        k = CK * c + kk
                        ins = v_.scalar_tensor_tensor(out=lo[:, k, :], in0=memory_bank(c)[:, kk * S:(kk + 1) * S],
                                                      scalar=mg[:, l, k:k + 1], in1=hi[:, k, :].bitcast(F32),
                                                      op0=ALU.mult, op1=ALU.subtract)
                ins.then_inc(freeB, 1)

            dve.wait_ge(mg_in, upto(mg_in, 16))
            memory_lo(0)
            split_lo(0, None)
            for n in range(PRO):
                if n + 1 < NC:
                    memory_lo(n + 1)
                if n == 0:
                    for k in range(1, AHEAD):
                        split_lo(k, None)
                if n == MEM_SQUARE[-1] + 1:
                    dve.wait_ge(sq_mem, upto(sq_mem, 1))
                    sum8(rm[:], ssm[:], 2).then_inc(rm_sum, 1)
                if n in TURN_P:
                    i = TURN_P[n]
                    turn_lo(None, NC + i, NC + i + 1, hhi, hlo, lambda k: col("ln", k), i)
                if n == 1:
                    split_lo(AHEAD, None)
                if 1 <= n < PRO - AHEAD:
                    split_lo(n + AHEAD, None)
                elif n > 0:
                    split_lo(n + AHEAD - PRO, 0)
                if n in KV_COPY:
                    ml = KV_COPY[n]
                    dve.wait_ge(sq_kv, upto(sq_kv, ml + 1))
                    sum8(sq8[:], kvT[:].rearrange("p a b -> p (a b)").rearrange("p (n d) -> p n d", d=HD), 8)\
                        .then_inc(kv_sum, 1)

            def frac_batch(l, b):
                upto = counter(l)
                if b == 0 and l == 0:
                    dve.wait_ge(used, upto(used, 0))
                elif b == 0:
                    dve.wait_ge(stepped, counter(l - 1)(stepped, NUM["glu1"] + 1))
                elif b >= 2:
                    dve.wait_ge(unrot, upto(unrot, TB * (b - 1)))
                h_ = tab[:, b % 2]
                for jj in range(TB):
                    ins = v_.tensor_scalar(h_[:, 0, jj, :], tvec[:], s5[:, 4, TB * b + jj:TB * b + jj + 1], None,
                                           ALU.mult)
                link(ins)
                link(v_.tensor_scalar(h_[:, 1], h_[:, 0], MAGIC, None, ALU.add))
                link(v_.tensor_scalar(h_[:, 1], h_[:, 1], MAGIC, None, ALU.subtract))
                v_.tensor_tensor(h_[:, 0], h_[:, 0], h_[:, 1], ALU.subtract).then_inc(frac, 1)

            for l in range(L):
                upto = counter(l)
                s5r = lambda i: s5[:, i, :]

                def topk_round(score):
                    link(v_.max(mx8[:], score))
                    link(v_.match_replace(score, mx8[:], score, TAKEN))

                def key_bias(dst, score, causal):
                    link(v_.scalar_tensor_tensor(out=dst, in0=score, scalar=0.5 * (NEG + TAKEN), in1=causal,
                                                 op0=ALU.is_le, op1=ALU.mult))
                    link(v_.tensor_scalar(dst, dst, 1.0, BIG, ALU.subtract, ALU.mult))

                for s in range(SLOTS):
                    g, c = divmod(s, NC)
                    if s in TURN_X:
                        turn_lo(l, BX + s - 2, s - 1, hhi, hlo, lambda k: col("ln", k), TURN_X[s])
                    if s in TURN_O:
                        co = TURN_O[s]
                        turn_lo(l, BO + co, 2 + co + 1, hhi, hlo, lambda k: col("on", k), co)
                    if s in TURN_N and l + 1 < L:
                        cn = TURN_N[s]
                        turn_lo(l, BN + cn, 10 + cn + 1, hhi, hlo, lambda k: col("ln", k), cn)
                    if s + AHEAD < SLOTS:
                        if s + AHEAD not in POOL_LO:
                            split_lo(s + AHEAD, l)
                    elif l + 1 < L:
                        split_lo(s + AHEAD - SLOTS, l + 1)
                    if s == 0 and l > 0:
                        x_add(l - 1, 3)
                    if s == 1:
                        dve.wait_ge(sq_x, upto(sq_x, 1))
                        sum8(rs[:], ssx[:], 2).then_inc(rs_sum, 1)
                    if s == 3:
                        dve.wait_ge(s5_exp, upto(s5_exp, 1))
                        are, aim = pa[:, PC["are"]:PC["are"] + ST], pa[:, PC["aim"]:PC["aim"] + ST]
                        v_.tensor_tensor(s5r(1), are, s5r(0), ALU.mult)
                        link(v_.tensor_tensor(s5r(2), aim, s5r(0), ALU.mult))
                        link(v_.tensor_scalar(s5r(2), s5r(2), 1.0 / TWO_PI, None, ALU.mult))
                        link(v_.tensor_scalar(s5r(3), s5r(2), MAGIC, None, ALU.add))
                        link(v_.tensor_scalar(s5r(3), s5r(3), MAGIC, None, ALU.subtract))
                        v_.tensor_tensor(s5r(4), s5r(2), s5r(3), ALU.subtract).then_inc(s5_phase, 1)
                    if s == 12:
                        dve.wait_ge(s5_sin, upto(s5_sin, 1))
                        if l > 0:
                            dve.wait_ge(x_out, upto(x_out, 0))
                        r_, sh, s1 = s5r(5), s5r(6), s5r(7)
                        link(v_.tensor_tensor(s5r(8), sh, sh, ALU.mult))
                        link(v_.tensor_tensor(s5r(9), r_, s5r(8), ALU.mult))
                        link(v_.tensor_scalar(s5r(10), r_, 1.0, None, ALU.subtract))
                        link(v_.scalar_tensor_tensor(out=s5r(10), in0=s5r(9), scalar=-2.0, in1=s5r(10), op0=ALU.mult,
                                                     op1=ALU.add))
                        v_.tensor_tensor(s5r(11), r_, s1, ALU.mult)
                        v_.tensor_tensor(s5r(8), are, are, ALU.mult)
                        link(v_.tensor_tensor(s5r(9), aim, aim, ALU.mult))
                        link(v_.tensor_tensor(s5r(8), s5r(8), s5r(9), ALU.add))
                        link(v_.reciprocal(s5r(8), s5r(8)))
                        for dst, a0, a1, op in ((12, 10, 11, ALU.add), (13, 11, 10, ALU.subtract)):
                            link(v_.tensor_tensor(s5r(9), s5r(a0), are, ALU.mult))
                            link(v_.tensor_tensor(s5r(14), s5r(a1), aim, ALU.mult))
                            link(v_.tensor_tensor(s5r(9), s5r(9), s5r(14), op))
                            link(v_.tensor_tensor(s5r(dst), s5r(9), s5r(8), ALU.mult))
                        fre, fim = (s5r(i).unsqueeze(2).to_broadcast([P, ST, 32]) for i in (12, 13))
                        tv = [t_[:].rearrange("p t d -> p (t d)").rearrange("p (j c) -> p j c", j=ST)
                              for t_ in (t1, t2, t3, kd)]
                        v_.tensor_tensor(tv[0], cp[:, :, 0, :], fre, ALU.mult)
                        v_.tensor_tensor(tv[1], cp[:, :, 1, :], fim, ALU.mult)
                        v_.tensor_tensor(tv[2], cp[:, :, 0, :], fim, ALU.mult)
                        link(v_.tensor_tensor(tv[3], cp[:, :, 1, :], fre, ALU.mult))
                        v_.tensor_tensor(cp[:, :, 0, :], tv[0], tv[1], ALU.subtract)
                        v_.scalar_tensor_tensor(out=cp[:, :, 1, :], in0=tv[2], scalar=-1.0, in1=tv[3], op0=ALU.mult,
                                                op1=ALU.subtract).then_inc(s5_c, 1)
                        dve.wait_ge(s5_c, upto(s5_c, 1))
                    if s in FRAC_SLOT:
                        frac_batch(l, FRAC_SLOT.index(s))
                    if s == SLOT["gate"]:
                        dve.wait_ge(stepped, upto(stepped, NUM["gate"] + 1))
                        bup = pa[:, PC["bup"]:PC["bup"] + S].unsqueeze(1).to_broadcast([P, NT, S])
                        v_.tensor_tensor(la[:], bank_of("gate")[:].rearrange("p (t d) -> p t d", t=NT), bup,
                                         ALU.add).then_inc(freeA[NUM["gate"] % 2], 1)
                    if s == 41:
                        dve.wait_ge(lsoft, upto(lsoft, 1))
                        v_.scalar_tensor_tensor(out=la[:], in0=la[:], scalar=0.0, in1=t1[:], op0=ALU.min,
                                                op1=ALU.subtract).then_inc(lsum, 1)
                    if s in AT and AT[s][:3] == "rel":
                        name = AT[s]
                        i = NUM[name] - NUM["rel1_0"]
                        dve.wait_ge(*result(upto, name))
                        if i == 0:
                            dve.wait_ge(roped_k, upto(roped_k, 1))
                        for hh in range(2 if i < 8 else 4):
                            if i < 8:
                                h_, t, w, dst, z = 2 * (i // 2 * 2 + hh) + i % 2, 1, S, sc[:], negm[:]
                            else:
                                h_, t, w, dst, z = 2 * ((i - 8) // 2 * 4 + hh) + i % 2, 0, P, sc0[:], negm[:, P:S]
                            ins = v_.scalar_tensor_tensor(
                                out=dst, in0=rel[:, i % 2, hh * w:(hh + 1) * w],
                                scalar=misc[:, t, MISC["iw"] + h_:MISC["iw"] + h_ + 1], in1=z if h_ == 0 else dst,
                                op0=ALU.mult, op1=ALU.add)
                            if hh < (1 if i < 8 else 3):
                                link(ins)
                        ins.then_inc(weighed, 1)
                        dve.wait_ge(weighed, upto(weighed, i + 1))
                    if s in TOP1:
                        topk_round(sc[:])
                    if s == TOP1[-1] + 1:
                        key_bias(bias1[:], sc[:], c01[:])
                    if s in TOP0:
                        topk_round(sc0[:])
                    if s == TOP0[-1] + 1:
                        key_bias(bias0[:], sc0[:], c01[:, P:S])
                    if s in NORM_SLOT:
                        n = NORM_SLOT.index(s)
                        dve.wait_ge(squared, upto(squared, n + 1))
                        if l + n >= 1:
                            dve.wait_ge(normr, upto(normr, n))
                        sum8(sq8[:], E3[:].rearrange("p t (h d) -> p (t h) d", d=HD), 8).then_inc(sq_read, 1)
                    if s in AT:
                        name = AT[s]
                        n = NUM[name]
                        b = bank_of(name)
                        fa = freeA[n % 2]
                        b4 = b[:].rearrange("p (h d) -> p h d", h=H)
                        if name in ("lg1_0", "lg1_1", "lg0"):
                            dve.wait_ge(stepped, upto(stepped, n + 1))
                            if name == "lg0":
                                dst, bv, bi, k = P0[:], b4, bias0, H
                            else:
                                i = int(name[-1])
                                dst, bv, bi, k = P1[:, 2 * i:2 * i + 2, :], b[:].rearrange("p (h d) -> p h d", h=2), bias1, 2
                            w = P if name == "lg0" else S
                            v_.scalar_tensor_tensor(out=dst, in0=bv, scalar=SCALE,
                                                    in1=bi[:].unsqueeze(1).to_broadcast([P, k, w]), op0=ALU.mult,
                                                    op1=ALU.add).then_inc(fa, 1)
                            if name == "lg1_1":
                                dve.wait_ge(*result(upto, "lg1_0"))
                                dve.wait_ge(*result(upto, "lg1_1"))
                                v_.tensor_reduce(nm1[:], P1[:], AX.X, ALU.max, negate=True).then_inc(biased1, 1)
                            if name == "lg0":
                                dve.wait_ge(*result(upto, "lg0"))
                                v_.tensor_reduce(nm0[:], P0[:], AX.X, ALU.max, negate=True).then_inc(biased0, 1)
                        if name in ("pv1", "pv0", "mv0", "mv1"):
                            t = int(name[2])
                            dve.wait_ge(stepped, upto(stepped, n + 1))
                            link(v_.reciprocal(ri[:], (su0, su1)[t][:]))
                            v_.tensor_tensor(obuf[:, B_DSA if name[0] == "p" else B_MEM, t, :]
                                             .rearrange("p (h d) -> p h d", h=H), b4,
                                             ri[:].unsqueeze(2).to_broadcast([P, H, HD]), ALU.mult).then_inc(fa, 1)
                            dve.wait_ge(*result(upto, name))
                        if name in ("at0", "at1"):
                            dve.wait_ge(stepped, upto(stepped, n + 1))
                            if name == "at1":
                                dve.wait_ge(stepped, upto(stepped, NUM["go0"] + 1))
                            v_.copy_predicated(attn[:], tri[:].bitcast(I32).unsqueeze(1).to_broadcast([P, H, P]), b4)\
                                .then_inc(fa, 1)
                        if name == "dS0":
                            dve.wait_ge(stepped, upto(stepped, n + 1))
                            dve.wait_ge(*result(upto, "dec"))
                            bv = b[:].rearrange("p (c h e) -> p c h e", c=2, h=2)
                            link(v_.tensor_copy(stt_[:, 0], bv[:, 0]))
                            for hp in range(2):
                                ins = v_.scalar_tensor_tensor(out=stt_[:, 1, hp, :], in0=stt_[:, 0, hp, :],
                                                              scalar=dec[:, hp, 1:2], in1=bv[:, 1, hp, :], op0=ALU.mult,
                                                              op1=ALU.add)
                            ins.then_inc(fa, 1)
                            dve.wait_ge(*result(upto, "dS0"))
                        if name == "dS1":
                            dve.wait_ge(stepped, upto(stepped, n + 1))
                            for hp in range(2):
                                ins = v_.scalar_tensor_tensor(out=stt_[:, 2, hp, :], in0=stt_[:, 1, hp, :],
                                                              scalar=dec[:, hp, 2:3], in1=b[:, hp * P:(hp + 1) * P],
                                                              op0=ALU.mult, op1=ALU.add)
                            ins.then_inc(fa, 1)
                        if name in ("go0", "go1"):
                            dve.wait_ge(stepped, upto(stepped, n + 1))
                            v_.tensor_copy(obuf[:, B_GLA, int(name[2]), :], b[:]).then_inc(fa, 1)
                        if name in ("cumD", "cumT", "cumL"):
                            dve.wait_ge(*result(upto, name))
                            if name == "cumD":
                                dve.wait_ge(taken, upto(taken, G_GQK + 1))
                            gq, gk = E2[:, :, 0:S], E2[:, :, S:2 * S]
                            if name == "cumD":
                                v_.scalar_tensor_tensor(out=t1[:], in0=gq, scalar=GD ** -0.5, in1=t1[:], op0=ALU.mult,
                                                        op1=ALU.mult)
                                v_.tensor_tensor(t2[:], gk, t2[:], ALU.mult).then_inc(gmul, 1)
                            elif name == "cumT":
                                v_.scalar_tensor_tensor(out=t3[:], in0=gq, scalar=GD ** -0.5, in1=t3[:], op0=ALU.mult,
                                                        op1=ALU.mult).then_inc(gmul, 1)
                            else:
                                v_.tensor_tensor(kd[:], gk, kd[:], ALU.mult).then_inc(gmul, 1)
                        if name[:2] == "ml":
                            t, i = int(name[2]), int(name[4])
                            dve.wait_ge(stepped, upto(stepped, n + 1))
                            nm = (nm0, nm1)[t][:, 2 * i:2 * i + 2]
                            link(v_.tensor_reduce(nm, b[:].rearrange("p (h d) -> p h d", h=2), AX.X, ALU.max, negate=True))
                            v_.tensor_scalar(nm, nm, SCALE, None, ALU.mult).then_inc(mmax, 1)
                        if name[:3] == "glu":
                            t = int(name[3])
                            dve.wait_ge(*result(upto, name))
                            dve.wait_ge(*result(upto, f"yt{t}"))
                            ins = v_.scalar_tensor_tensor(out=obuf[:, B_S5, t, :], in0=gt[:, t, :], scalar=1.0,
                                                          in1=obuf[:, B_S5, t, :], op0=ALU.add, op1=ALU.mult)
                            if t == 1:
                                ins.then_inc(obr, 1)
                    if s in BU:
                        j = BU[s]
                        b, jj = divmod(j, TB)
                        dve.wait_ge(wroteB, upto(wroteB, BBU + j + 1))
                        if jj == 0:
                            dve.wait_ge(phased, upto(phased, b + 1))
                        bb = bankB[:].rearrange("p (i s) -> p i s", i=2)
                        for i in (1, 0):
                            ins = v_.tensor_tensor(rot[:, i], bb, tab[:, b % 2, i, jj, :].unsqueeze(1)
                                                   .to_broadcast([P, 2, S]), ALU.mult)
                        ins.then_inc(freeB, 1)
                        dve.wait_ge(freeB, upto(freeB, BBU + j + 1))
                        if j >= 2:
                            dve.wait_ge(unrot, upto(unrot, j - 1))
                        z = vz[:, j % 2]
                        v_.tensor_tensor(z[:, 0], rot[:, 1, 0], rot[:, 0, 1], ALU.add)
                        link(v_.tensor_tensor(z[:, 1], rot[:, 1, 1], rot[:, 0, 0], ALU.subtract))
                        for i in range(2):
                            ins = v_.tensor_tensor_scan(z[:, i], s5[:, 5, j:j + 1].to_broadcast([P, S]), z[:, i], 0.0,
                                                        ALU.mult, ALU.add)
                        ins.then_inc(scanned, 1)
                    for ct in range(4):
                        base = S5_SLOT[4 * ct + 3] + S5_LAG
                        y = ych[:, ct, :]
                        if s == base:
                            dve.wait_ge(yprod, upto(yprod, 4 * ct + 4))
                            if l == 0 and ct == 0:
                                dve.wait_ge(k_out[1], 16)
                            link(v_.scalar_tensor_tensor(out=y, in0=uT[:, ct, :], scalar=col("d", ct),
                                                         in1=bankY[:, ct % 2, :], op0=ALU.mult, op1=ALU.add))
                            link(v_.tensor_tensor(ytmp[:], y, y, ALU.mult))
                            v_.scalar_tensor_tensor(out=ytmp[:], in0=ytmp[:], scalar=1 / GELU_CUBE, in1=y, op0=ALU.add,
                                                    op1=ALU.mult).then_inc(ypoly, 1)
                        if s == base + 2:
                            dve.wait_ge(ytanh, upto(ytanh, ct + 1))
                            v_.scalar_tensor_tensor(out=y, in0=ytmp[:], scalar=1.0, in1=y, op0=ALU.add,
                                                    op1=ALU.mult).then_inc(gelud, 1)
                            dve.wait_ge(gelud, upto(gelud, ct + 1))
                    if c == 0 and G_Z < g <= G_OUT:
                        z = g - G_Z - 1
                        dve.wait_ge(ztanh, upto(ztanh, z + 1))
                        for t in range(NT):
                            ins = v_.scalar_tensor_tensor(out=Ez[:, t, :], in0=Ez[:, t, :], scalar=1.0,
                                                          in1=acc[(g - 1) % 2][t][:], op0=ALU.add, op1=ALU.mult)
                        ins.then_inc(gated, 1)
                        dve.wait_ge(gated, upto(gated, z + 1))
                    if s in ZMUL_SLOT:
                        z = ZMUL_SLOT.index(s)
                        dve.wait_ge(normr, upto(normr, {B_DSA: SQ_DSA, B_GLA: SQ_GLA, B_S5: SQ_S5, B_MEM: SQ_MEM}[z] + 1))
                        for t in range(NT):
                            ins = v_.scalar_tensor_tensor(out=obuf[:, z, t, :], in0=Ez[:, t, :], scalar=rsh[:, t:t + 1],
                                                          in1=obuf[:, z, t, :], op0=ALU.mult, op1=ALU.mult)
                        ins.then_inc(zmul, 1)
                    if s in (104, 112, 120):
                        x_add(l, (s - 104) // 8)
            dve.wait_ge(x_in, counter(L - 1)(x_in, 64))
            for t in range(NT):
                if t == 0:
                    dve.wait_ge(tile_done, 1)
                else:
                    dve.wait_ge(used, counter(L - 1)(used, SLOTS))
                v_.tensor_tensor(xr[:, 0, t, :], acc[1][t][:], xr[:, 0, t, :], ALU.add).then_inc(last_added, 1)


def kernel(**inputs):
    import numpy as _np
    import concourse.bacc as _bacc
    from concourse import mybir as _mybir
    from concourse.bass_utils import run_bass_kernel_spmd as _run

    a = {k: _np.asarray(v) for k, v in inputs.items()}

    def chunks(w, k0=0):
        w = _np.concatenate([w, _np.zeros((D, W - w.shape[1]), w.dtype)], 1)
        return w.reshape(NC, CK, P, W).transpose(0, 2, 1, 3).reshape(NC, P, CK * W)

    parts = []
    for l in range(L):
        parts += [chunks(a["w_mem_kv"][l][:, :W]), chunks(a["w_mem_kv"][l][:, W:])]
    rows = _np.r_[1024:1536, 0:512, 512:1024, 1536:2048]
    for l in range(L):
        w = a["w_in"][l]

        def cut(name, n):
            return w[:, IN[name]:IN[name] + n]
        for p in (cut("su", W), cut("iq", W), w[:, IN["iq"] + W:IN["iq"] + 2 * W],
                  _np.concatenate([cut("dk", 256), cut("ik", 64), cut("iw", 16), cut("glr", 16)], 1),
                  cut("dq", W), cut("gq", W), cut("gv", W), cut("mq", W),
                  cut("dz", W), cut("gz", W), cut("sz", W), cut("mz", W)):
            parts.append(chunks(p))
        wo = a["w_out"][l][rows]
        parts += [chunks(wo[:, i * W:(i + 1) * W]) for i in range(4)]
    stream = _np.concatenate(parts, 0)

    def rows_of(v):
        return v.reshape(-1, P).T

    def states(v):
        return v.reshape(ST, P).T

    def wide(v):
        return _np.broadcast_to(v, (P, v.shape[0]))
    par = _np.stack([_np.concatenate([
        rows_of(a["ln_gain"][l]), rows_of(a["out_norm"][l][rows]), states(a["s5_a_re"][l]), states(a["s5_a_im"][l]),
        states(_np.broadcast_to(a["s5_log_step"][l][:, None], (32, 64))), rows_of(a["s5_d"][l]),
        a["mem_q_norm"][l][:, None], wide(a["dsa_q_norm"][l]), wide(a["dsa_k_norm"][l]), wide(a["gla_b_up"][l])], 1)
        for l in range(L)])
    mgain = _np.stack([_np.concatenate([rows_of(a["mem_norm"][l]), a["mem_k_norm"][l][:, None]], 1)
                       for l in range(L)], 1)
    bmat = _np.zeros((L, P, 4, 2, P), _np.float32)
    cmat = _np.zeros((L, P, ST, 2, 32), _np.float32)
    for i, (bn, cn) in enumerate((("s5_b_re", "s5_c_re"), ("s5_b_im", "s5_c_im"))):
        for gg in range(2):
            b = a[bn].reshape(L, 4, 4, 2, 64, 16)[:, :, :, gg]
            for jj in range(4):
                r = 32 * jj + 16 * gg
                bmat[:, r:r + 16, :, i, 64 * gg:64 * gg + 64] = b[:, :, jj].transpose(0, 3, 1, 2)
            c = a[cn].reshape(L, ST, 2, 16, 64)[:, :, gg]
            cmat[:, 64 * gg:64 * gg + 64, :, i, 16 * gg:16 * gg + 16] = c.transpose(0, 3, 1, 2)
    wglu = a["s5_w_glu"].reshape(L, 4, P, W).transpose(0, 2, 1, 3).reshape(L, P, 4 * W)
    invf = _np.concatenate([_np.float32(500000.0) ** (-_np.arange(n, dtype=_np.float32) * _np.float32(2.0)
                                                      / _np.float32(2 * n)) for n in (8, 16)]).astype(_np.float32)
    pos = a["positions"].reshape(NT, P).T
    sent = dict(stream=stream, mem=a["mem"][0], x=a["x"][0], pos=pos, invf=invf, mgain=mgain, par=par, bmat=bmat,
                cmat=cmat, wup=a["gla_w_up"], wglu=wglu)
    sent = {k: _np.ascontiguousarray(v) for k, v in sent.items()}

    nc = _bacc.Bacc("TRN2", target_bir_lowering=False, num_devices=1)
    args = {k: nc.dram_tensor(f"in_{k}", v.shape, _mybir.dt.from_np(v.dtype), kind="ExternalInput").ap()
            for k, v in sent.items()}
    out = nc.dram_tensor("out_0", (S, D), _mybir.dt.float32, kind="ExternalOutput").ap()
    build(nc, out=out, **args)
    r = _run(nc, [{f"in_{k}": v for k, v in sent.items()}], core_ids=[0])
    return r.results[0]["out_0"].reshape(a["x"].shape)
```
